# Optimizing a Trainium2 kernel written in Bass

```python
import math
import jax, jax.numpy as jnp
from jax import lax
import numpy as np

D_MODEL = 1024
BATCH = 1
SEQ = 512
DEPTH = 2

N_A_LAYERS = DEPTH // 2
N_B_LAYERS = DEPTH - N_A_LAYERS
CONV_WIDTH = 31
D_FF = 2816
FFN_CONV_WIDTH = 3
N_HEADS = 8
HEAD_DIM = 64
V_DIM = 2 * HEAD_DIM
Q_BLOCK = 128
EPS = 1e-6
NEG_INF = -1e30

kernel_name = "yoco_conformer_diffattn_convffn"

def lambda_init_fn(layer_idx):
    return 0.8 - 0.6 * math.exp(-0.3 * layer_idx)

def rms_norm(x, g):
    xf = x.astype(jnp.float32)
    y = xf * lax.rsqrt(jnp.mean(xf * xf, axis=-1, keepdims=True) + EPS)
    return (y * g.astype(jnp.float32)).astype(x.dtype)

def layer_norm(x, g, b):
    xf = x.astype(jnp.float32)
    mu = jnp.mean(xf, axis=-1, keepdims=True)
    xc = xf - mu
    y = xc * lax.rsqrt(jnp.mean(xc * xc, axis=-1, keepdims=True) + EPS)
    return (y * g.astype(jnp.float32) + b.astype(jnp.float32)).astype(x.dtype)

def causal_depthwise_conv(u, w, b):
    width, c = w.shape
    y = lax.conv_general_dilated(
        u, w.reshape(width, 1, c).astype(u.dtype), window_strides=(1,),
        padding=[(width - 1, 0)], dimension_numbers=('NWC', 'WIO', 'NWC'),
        feature_group_count=c)
    return y + b.astype(u.dtype)

def conformer_conv_module(x, norm_g, pw1_w, pw1_b, dw_w, dw_b, ln_g, ln_b, pw2_w, pw2_b):
    h = rms_norm(x, norm_g)
    u = h @ pw1_w + pw1_b
    u = u[..., :D_MODEL] * jax.nn.sigmoid(u[..., D_MODEL:])
    u = causal_depthwise_conv(u, dw_w, dw_b)
    u = jax.nn.silu(layer_norm(u, ln_g, ln_b))
    return x + u @ pw2_w + pw2_b

def conv_ffn(x, norm_g, w_in, dw_w, dw_b, w_out):
    h = rms_norm(x, norm_g)
    u = causal_depthwise_conv(h @ w_in, dw_w, dw_b)
    gate, up = u[..., :D_FF], u[..., D_FF:]
    return x + (jax.nn.silu(gate) * up) @ w_out

def diff_attention(q, k, v, lam):
    b, s = q.shape[0], q.shape[1]
    nb = s // Q_BLOCK
    scale = HEAD_DIM ** -0.5
    q_blocks = jnp.moveaxis(q.reshape(b, nb, Q_BLOCK, N_HEADS, 2, HEAD_DIM), 1, 0)
    key_pos = jnp.arange(s)
    vf = v.astype(jnp.float32)

    def one_block(args):
        qb, start = args
        scores = jnp.einsum('bqhcd,bkhcd->bhcqk', qb, k,
                            preferred_element_type=jnp.float32) * scale
        q_pos = start + jnp.arange(Q_BLOCK)
        causal = key_pos[None, :] <= q_pos[:, None]
        probs = jax.nn.softmax(jnp.where(causal, scores, NEG_INF), axis=-1)
        diff = probs[:, :, 0] - lam * probs[:, :, 1]
        return jnp.einsum('bhqk,bkhe->bqhe', diff, vf)

    out = lax.map(one_block, (q_blocks, jnp.arange(nb) * Q_BLOCK))
    return jnp.moveaxis(out, 0, 1).reshape(b, s, N_HEADS, V_DIM)

def setup_inputs(seed: int = 0) -> dict:
    key = jax.random.key(seed)
    ks = iter(jax.random.split(key, 40))

    def nrm(shape, scale):
        return jax.random.normal(next(ks), shape, jnp.float32) * scale

    def gain(shape):
        return 1.0 + 0.05 * jax.random.normal(next(ks), shape, jnp.float32)

    na, nbl, d = N_A_LAYERS, N_B_LAYERS, D_MODEL
    qk_width = N_HEADS * 2 * HEAD_DIM
    v_width = N_HEADS * V_DIM
    return {
        "x": nrm((BATCH, SEQ, d), 1.0),
        "conv_norm_g": gain((na, d)),
        "conv_pw1_w": nrm((na, d, 2 * d), d ** -0.5),
        "conv_pw1_b": nrm((na, 2 * d), 0.02),
        "conv_dw_w": nrm((na, CONV_WIDTH, d), CONV_WIDTH ** -0.5),
        "conv_dw_b": nrm((na, d), 0.02),
        "conv_ln_g": gain((na, d)),
        "conv_ln_b": nrm((na, d), 0.02),
        "conv_pw2_w": nrm((na, d, d), d ** -0.5),
        "conv_pw2_b": nrm((na, d), 0.02),
        "kv_norm_g": gain((d,)),
        "w_k": nrm((d, qk_width), d ** -0.5),
        "w_v": nrm((d, v_width), d ** -0.5),
        "k_norm_g": gain((HEAD_DIM,)),
        "attn_norm_g": gain((nbl, d)),
        "w_q": nrm((nbl, d, qk_width), d ** -0.5),
        "q_norm_g": gain((nbl, HEAD_DIM)),
        "lambda_q1": nrm((nbl, HEAD_DIM), 0.1),
        "lambda_k1": nrm((nbl, HEAD_DIM), 0.1),
        "lambda_q2": nrm((nbl, HEAD_DIM), 0.1),
        "lambda_k2": nrm((nbl, HEAD_DIM), 0.1),
        "subln_g": gain((nbl, V_DIM)),
        "w_o": nrm((nbl, v_width, d), v_width ** -0.5),
        "ffn_norm_g": gain((DEPTH, d)),
        "ffn_w_in": nrm((DEPTH, d, 2 * D_FF), d ** -0.5),
        "ffn_dw_w": nrm((DEPTH, FFN_CONV_WIDTH, 2 * D_FF), FFN_CONV_WIDTH ** -0.5),
        "ffn_dw_b": nrm((DEPTH, 2 * D_FF), 0.02),
        "ffn_w_out": nrm((DEPTH, D_FF, d), D_FF ** -0.5),
    }

def reference(x, conv_norm_g, conv_pw1_w, conv_pw1_b, conv_dw_w, conv_dw_b, conv_ln_g, conv_ln_b,
              conv_pw2_w, conv_pw2_b, kv_norm_g, w_k, w_v, k_norm_g, attn_norm_g, w_q, q_norm_g,
              lambda_q1, lambda_k1, lambda_q2, lambda_k2, subln_g, w_o, ffn_norm_g, ffn_w_in,
              ffn_dw_w, ffn_dw_b, ffn_w_out):
    b, s, _ = x.shape
    for layer in range(DEPTH):
        if layer < N_A_LAYERS:
            i = layer
            x = conformer_conv_module(x, conv_norm_g[i], conv_pw1_w[i], conv_pw1_b[i], conv_dw_w[i],
                                      conv_dw_b[i], conv_ln_g[i], conv_ln_b[i], conv_pw2_w[i],
                                      conv_pw2_b[i])
        else:
            j = layer - N_A_LAYERS
            if j == 0:
                hk = rms_norm(x, kv_norm_g)
                k_sh = rms_norm((hk @ w_k).reshape(b, s, N_HEADS, 2, HEAD_DIM), k_norm_g)
                v_sh = (hk @ w_v).reshape(b, s, N_HEADS, V_DIM)
            lam_init = lambda_init_fn(layer)
            lam = (jnp.exp(jnp.sum(lambda_q1[j].astype(jnp.float32) * lambda_k1[j].astype(jnp.float32)))
                   - jnp.exp(jnp.sum(lambda_q2[j].astype(jnp.float32) * lambda_k2[j].astype(jnp.float32)))
                   + lam_init)
            h = rms_norm(x, attn_norm_g[j])
            q = rms_norm((h @ w_q[j]).reshape(b, s, N_HEADS, 2, HEAD_DIM), q_norm_g[j])
            o = diff_attention(q, k_sh, v_sh, lam)
            o = rms_norm(o, subln_g[j]) * (1.0 - lam_init)
            x = x + (o.reshape(b, s, N_HEADS * V_DIM) @ w_o[j].astype(jnp.float32)).astype(x.dtype)
        x = conv_ffn(x, ffn_norm_g[layer], ffn_w_in[layer], ffn_dw_w[layer], ffn_dw_b[layer],
                     ffn_w_out[layer])
    return x


_drawn_inputs = setup_inputs


def setup_inputs(seed=0):
    import zlib

    import numpy as np

    out = dict(_drawn_inputs(seed))
    spreads = {}
    factors = {'conv_ln_b': 2.674,
     'k_norm_g': 3.409,
     'attn_norm_g': 3.393,
     'q_norm_g': 2.799,
     'lambda_k1': 4.885,
     'lambda_q2': 5.458,
     'lambda_k2': 8.0,
     'ffn_dw_b': 2.812}
    for name, (base, spread) in spreads.items():
        noise = np.random.default_rng([zlib.crc32(name.encode()), seed]).standard_normal(out[name].shape)
        drawn = base * np.exp(spread * noise) if base else spread * noise
        out[name] = __import__('jax').numpy.asarray(drawn.astype(out[name].dtype))
    for name, factor in factors.items():
        out[name] = (out[name] * factor).astype(out[name].dtype)
    return out
```

```python
import math
from contextlib import ExitStack, contextmanager

import numpy as np

import concourse.bass as bass
from concourse import mybir

F32 = mybir.dt.float32
F32R = mybir.dt.float32r
BF16 = mybir.dt.bfloat16
ALU = mybir.AluOpType
ACT = mybir.ActivationFunctionType
AX_X = mybir.AxisListType.X

P = 128
D = 1024
SEQ = 512
KT = D // P
TB = SEQ // P
TAPS = 31
D_FF = 2816
FT = D_FF // P
FTAPS = 3
HEADS = 8
HD = 64
VD = 2 * HD
EPS = 1e-6
NEG = -1e30
LAM_INIT = 0.8 - 0.6 * math.exp(-0.3)
RING = 2
SLOT = KT * 2 * P
TILE0 = 2
CHUNKS = [KT, KT, FT - 2 * KT]

PARAM_WIDTHS = [
    ("conv_norm_g", KT), ("pw1_b", 2 * KT), ("dw_w", KT * TAPS), ("dw_b", KT), ("ln_g", KT), ("ln_b", KT),
    ("pw2_b", KT), ("kv_norm_g", KT), ("attn_norm_g", KT), ("ffn_norm_g", 2 * KT), ("ffn_dw_w", 2 * 2 * FT * FTAPS),
    ("ffn_dw_b", 2 * 2 * FT), ("k_norm_g", 1), ("q_norm_g", 1), ("subln_g", 1),
]
PARAM_AT = {}
N_PARAMS = 0
for _name, _width in PARAM_WIDTHS:
    PARAM_AT[_name] = N_PARAMS
    N_PARAMS += _width


def unit_plan():
    first, widths = {}, []

    def phase(name, count, width=SLOT):
        first[name] = len(widths)
        widths.extend([width] * count)

    def ffn(layer):
        for c, tiles in enumerate(CHUNKS):
            phase(("in", layer, c), tiles)
            phase(("out", layer, c), KT // 2, tiles * 2 * P)

    phase("pw1", KT)
    phase("pw2", KT // 2)
    ffn(0)
    for name in "vkq":
        phase(name, KT // 2)
    phase("wo", KT // 2)
    ffn(1)
    starts = [sum(widths[:n]) for n in range(len(widths) + 1)]
    return first, widths, starts


FIRST, WIDTHS, STARTS = unit_plan()
UNITS = len(WIDTHS)


class Own:

    def __init__(self, engine, semaphore):
        self.engine, self.semaphore, self.base, self.count = engine, semaphore, 0, 0

    def mark(self, instruction):
        instruction.then_inc(self.semaphore, 1)
        self.count += 1
        return self.count

    def wait(self, count):
        self.engine.wait_ge(self.semaphore, self.base + count)

    @contextmanager
    def loop(self, times, each):
        before = self.base + self.count
        with self.engine.Fori(0, times) as i:
            self.base, self.count = before + each * i, 0
            yield i
            assert self.count == each, (self.count, each)
        self.base, self.count = before + each * times, 0


def trunk(nc, x_t, stream, params, lambdas, out_t):
    with ExitStack() as ctx:
        def sb(name, shape, dtype=F32):
            return ctx.enter_context(nc.sbuf_tensor(name, shape, dtype))

        def sem(name):
            return ctx.enter_context(nc.semaphore(name))

        x = sb("x", [P, KT, SEQ])
        xg_hi = sb("xg_hi", [P, KT, SEQ], F32R)
        xg_lo = sb("xg_lo", [P, KT, SEQ], F32R)
        w_raw = sb("w_raw", [P, RING, SLOT])
        w_hi = sb("w_hi", [P, RING, SLOT], F32R)
        w_lo = sb("w_lo", [P, RING, SLOT], F32R)
        par = sb("par", [P, N_PARAMS])
        ident = sb("ident", [P, P])
        ident16 = sb("ident16", [P, P], BF16)
        mask16 = sb("mask16", [P, P], BF16)
        small = sb("small", [P, 96])
        eps = small[:, 0:1]
        gq8 = small[:, 1:2]
        gsub = small[:, 2:3]
        neg_lam = small[:, 3:4]
        lam_sum = small[:, 4:6]
        lam_exp = small[:, 6:8]
        rs_t = small[:, 8:12]
        rs_t_in = small[:, 12:16]
        neg_max = small[:, 16:24]
        prob_sum = small[:, 24:32]
        inv = small[:, 32:40]
        lam_inv = small[:, 40:44]
        o_ms = small[:, 44:48]
        o_in = small[:, 48:52]
        o_rs = small[:, 52:56]
        half = small[:, 56:57]

        area_r = sb("area_r", [P, 14 * 1024], F32R)
        area_f = sb("area_f", [P, 12 * 1024 + 64])

        def cut(area, at, *shape):
            n = math.prod(shape)
            v = area[:, at:at + n]
            if len(shape) == 2:
                v = v.rearrange("p (a b) -> p a b", a=shape[0])
            if len(shape) == 3:
                v = v.rearrange("p (a b c) -> p a b c", a=shape[0], b=shape[1])
            return v

        sq = cut(area_f, 10240, 2, SEQ)
        sq_sum = cut(area_f, 11264, SEQ)
        act_hi = cut(area_r, 0, KT, SEQ)
        act_lo = cut(area_r, 4096, KT, SEQ)
        rs = cut(area_f, 9216, SEQ)
        ms = cut(area_f, 9728, SEQ)
        UP = SEQ + FTAPS - 1
        ffn_u = cut(area_f, 0, 4, UP)
        ffn_t = cut(area_f, 2304, 4, SEQ)
        CP = SEQ + TAPS - 1
        conv_u = cut(area_f, 0, 2, CP)
        conv_a = cut(area_f, 1088, 2, SEQ)
        conv_b = cut(area_f, 2112, SEQ)
        conv_c = cut(area_f, 2624, KT, SEQ)
        ln_mean = cut(area_f, 6720, SEQ)
        ln_sq = cut(area_f, 7232, 2, SEQ)
        ln_sum = cut(area_f, 8256, SEQ)
        v_hi = cut(area_r, 0, TB, D)
        v_lo = cut(area_r, 4096, TB, D)
        kT_hi = cut(area_r, 8192, SEQ)
        kT_lo = cut(area_r, 8704, SEQ)
        qT_hi = cut(area_r, 9216, SEQ)
        qT_lo = cut(area_r, 9728, SEQ)
        dT_hi = cut(area_r, 10240, TB, SEQ)
        dT_lo = cut(area_r, 12288, TB, SEQ)
        k_sb = cut(area_f, 0, TB, D)
        q_sb = cut(area_f, 4096, TB, D)
        kn = cut(area_f, 8192, TB, P)
        qn = cut(area_f, 8704, TB, P)
        o_sb = cut(area_f, 9216, TB, VD)
        o_sq = cut(area_f, 9728, TB, VD)
        prob = cut(area_f, 10240, 2, 2, SEQ)
        kq_sq = cut(area_f, 8192, 2, SEQ)
        stat = sb("stat", [P, 2, TB, 2 * HEADS])
        stat_in = sb("stat_in", [P, 2, TB, 2 * HEADS])
        stat_rs = sb("stat_rs", [P, 2, TB, 2 * HEADS])
        lam_in = area_f[:, 8768:8768 + 4 * HD].rearrange("p (a b) -> p a b", a=4)
        lam_prod = area_f[:, 9024:9024 + 2 * HD].rearrange("p (a b) -> p a b", a=2)
        ones = sb("ones", [P, P])

        bank = [ctx.enter_context(nc.psum_tensor(f"bank{n}", [P, SEQ], F32)) for n in range(8)]
        NORM = 7

        par_in = sem("par_in")
        lam_in_sem = sem("lam_in")
        x_in = [sem(f"x_in{n}") for n in range(KT)]
        w_in = [sem(f"w_in{n}") for n in range(RING)]
        w_hi_done = sem("w_hi_done")
        w_lo_done = sem("w_lo_done")
        tiles = sem("tiles")
        banks_free = sem("banks_free")
        const_ready = sem("const_ready")
        lam_summed = sem("lam_summed")
        lam_exped = sem("lam_exped")
        dve_own = sem("dve_own")
        pool_own = sem("pool_own")
        dve_const = sem("dve_const")
        x_new = sem("x_new")
        xg_hi_done = sem("xg_hi_done")
        xg_lo_done = sem("xg_lo_done")
        sq_done = sem("sq_done")
        sq_added = sem("sq_added")
        norm_mm = sem("norm_mm")
        norm_ms = sem("norm_ms")
        norm_rs = sem("norm_rs")
        u_done = sem("u_done")
        tap0 = sem("tap0")
        taps_done = sem("taps_done")
        silu_done = sem("silu_done")
        prod_done = sem("prod_done")
        a_hi_done = sem("a_hi_done")
        a_lo_done = sem("a_lo_done")
        c_g = sem("c_g")
        c_sig = sem("c_sig")
        c_u = sem("c_u")
        c_tap = sem("c_tap")
        c_done = sem("c_done")
        c_added = sem("c_added")
        mean_mm = sem("mean_mm")
        mean_sb = sem("mean_sb")
        xc_done = sem("xc_done")
        xc_sq = sem("xc_sq")
        var_mm = sem("var_mm")
        var_ms = sem("var_ms")
        var_rs = sem("var_rs")
        y_n = sem("y_n")
        y_s = sem("y_s")
        xb = sem("xb")
        v_hi_s = sem("v_hi_s")
        kq_sum = sem("kq_sum")
        kq_root = sem("kq_root")
        kq_rs = sem("kq_rs")
        n_done = sem("n_done")
        tr_done = sem("tr_done")
        kT_h = sem("kT_h")
        kT_l = sem("kT_l")
        s_done = sem("s_done")
        m_done = sem("m_done")
        e_done = sem("e_done")
        d_done = sem("d_done")
        dt_done = sem("dt_done")
        dT_h = sem("dT_h")
        dT_l = sem("dT_l")
        o_done = sem("o_done")
        o_sum = sem("o_sum")
        o_rs_s = sem("o_rs_s")
        on_done = sem("on_done")
        oT_done = sem("oT_done")
        oT_h = sem("oT_h")
        oT_l = sem("oT_l")
        out_s = sem("out_s")

        def p(name, n=0, width=1):
            at = PARAM_AT[name] + n
            return par[:, bass.ds(at, width)]

        stages = ["conv", "ffn0", "kv", "ffn1"]
        gains = {"conv": ("conv_norm_g", 0), "ffn0": ("ffn_norm_g", 0), "kv": ("kv_norm_g", 0), "ffn1": ("ffn_norm_g", KT)}
        XG = {"conv": 0, "ffn0": KT, "kv": 2 * KT, "attn": 3 * KT, "ffn1": 4 * KT}
        SQ = {"conv": 0, "ffn0": KT, "kv": 2 * KT, "ffn1": 3 * KT}

        def operand(stage):
            return (act_hi, act_lo) if stage == "ffn1" else (xg_hi, xg_lo)

        def products(layer):
            return (xg_hi, xg_lo) if layer else (act_hi, act_lo)

        block = ctx.enter_context(nc.Block())

        @block.sync
        def _(sp):
            sp.dma_start(par[:, :], params).then_inc(par_in, 16)
            sp.dma_start(lam_in, lambdas).then_inc(lam_in_sem, 16)
            for k in range(KT):
                sp.dma_start(x[:, k, :], x_t[k * P:(k + 1) * P, :]).then_inc(x_in[k], 16)
                if k < RING:
                    sp.dma_start(w_raw[:, k, :], stream[:, STARTS[k]:STARTS[k + 1]]).then_inc(w_in[k], 16)
            n = RING
            while n < UNITS:
                width = WIDTHS[n]
                count = 1
                while n + count < UNITS and WIDTHS[n + count] == width:
                    count += 1
                assert n % RING == 0 and count % RING == 0
                with sp.Fori(0, count // RING) as i:
                    for j in range(RING):
                        sp.wait_ge(w_lo_done, n + j - RING + 1 + RING * i)
                        sp.dma_start(w_raw[:, j, 0:width],
                                     stream[:, bass.ds(STARTS[n] + j * width + RING * width * i, width)]
                                     ).then_inc(w_in[j], 16)
                n += count
            for k in range(KT):
                sp.wait_ge(x_new, 3 * KT + k + 1)
                sp.dma_start(out_t[k * P:(k + 1) * P, :], x[:, k, :]).then_inc(out_s, 16)
            sp.wait_ge(out_s, 16 * KT)

        @block.gpsimd
        def _(pool):
            own = Own(pool, pool_own)
            own.mark(pool.memset(ident[:, :], 0.0))
            own.mark(pool.memset(ident16[:, :], 0.0))
            n = own.mark(pool.memset(mask16[:, :], 0.0))
            own.wait(n)
            pool.affine_select(out=ident[:, :], in_=ident[:, :], compare_op=ALU.not_equal, fill=1.0, base=0,
                               pattern=[[-1, P]], channel_multiplier=1).then_inc(const_ready, 1)
            pool.affine_select(out=ident16[:, :], in_=ident16[:, :], compare_op=ALU.not_equal, fill=1.0, base=0,
                               pattern=[[-1, P]], channel_multiplier=1).then_inc(const_ready, 1)
            pool.affine_select(out=mask16[:, :], in_=mask16[:, :], compare_op=ALU.is_ge, fill=NEG, base=0,
                               pattern=[[-1, P]], channel_multiplier=1).then_inc(const_ready, 1)
            pool.memset(half[:, :], -0.5).then_inc(const_ready, 1)
            pool.wait_ge(const_ready, 4)

            def sum_squares(stage):
                at = SQ[stage]
                for k in range(KT):
                    pool.wait_ge(sq_done, at + k + 1)
                    if k == 0:
                        pool.tensor_copy(sq_sum, sq[:, k % 2, :]).then_inc(sq_added, 1)
                    else:
                        pool.wait_ge(sq_added, 2 + at + k)
                        pool.tensor_tensor(sq_sum, sq_sum, sq[:, k % 2, :], ALU.add).then_inc(sq_added, 1)

            def power(out, in_, shape):
                return pool.tensor_tensor(out, in_, half.broadcast_to(shape), ALU.pow)

            sum_squares("conv")
            for k in range(KT):
                pool.wait_ge(c_done, k + 1)
                if k == 0:
                    pool.tensor_copy(ln_sum, conv_c[:, k, :]).then_inc(c_added, 1)
                else:
                    pool.wait_ge(c_added, k)
                    pool.tensor_tensor(ln_sum, ln_sum, conv_c[:, k, :], ALU.add).then_inc(c_added, 1)
            sum_squares("ffn0")
            sum_squares("kv")
            with pool.Fori(0, HEADS) as h:
                pool.wait_ge(o_sum, h + 1)
                power(o_rs, o_in, [P, TB]).then_inc(o_rs_s, 1)
            sum_squares("ffn1")

        @block.scalar
        def _(act):
            def split_weights(n, j):
                act.wait_ge(w_in[j], (n - j) * (16 // RING) + 16)
                act.wait_ge(tiles, TILE0 + 2 * n - 2)
                act.activation(w_hi[:, j, :], w_raw[:, j, :], ACT.Copy).then_inc(w_hi_done, 1)

            def xg_tile(stage, k, square=True):
                name, at = gains[stage] if stage in gains else ("attn_norm_g", 0)
                act.activation(operand(stage)[0][:, k, :], x[:, k, :], ACT.Copy, scale=p(name, at + k)).then_inc(xg_hi_done, 1)
                if square:
                    act.wait_ge(sq_added, SQ[stage] + k + 1)
                    act.activation(sq[:, k % 2, :], x[:, k, :], ACT.Square).then_inc(sq_done, 1)

            def mean_square(stage_n):
                act.wait_ge(norm_mm, stage_n + 1)
                act.activation(ms, bank[NORM][:, :], ACT.Sqrt, bias=eps, scale=1.0 / D).then_inc(norm_ms, 1)

            act.wait_ge(par_in, 16)
            act.wait_ge(dve_const, 1)
            act.wait_ge(lam_summed, 1)
            act.activation(lam_exp, lam_sum, ACT.Exp).then_inc(lam_exped, 1)
            for k in range(KT):
                act.wait_ge(x_in[k], 16)
                xg_tile("conv", k)
                if k == 1:
                    split_weights(0, 0)
            mean_square(0)

            def conv_unit(m, j, n):
                split_weights(n + 1, 1 - j)
                act.wait_ge(c_g, m + 1)
                act.activation(conv_a[:, 1, :], conv_a[:, 1, :], ACT.Sigmoid, bias=p("pw1_b", KT + m)).then_inc(c_sig, 1)
                act.wait_ge(c_u, m + 1)
                act.activation(conv_b, conv_u[:, j, 0:SEQ], ACT.Identity, bias=p("dw_b", m),
                               scale=p("dw_w", m * TAPS)).then_inc(c_tap, 1)

            with act.Fori(0, KT // 2) as i:
                for j in range(2):
                    conv_unit(2 * i + j, j, 2 * i + j)

            act.wait_ge(mean_mm, 1)
            act.activation(ln_mean, bank[NORM][:, :], ACT.Copy, scale=1.0 / D).then_inc(mean_sb, 1)
            for k in range(KT):
                act.wait_ge(xc_done, k + 1)
                if k >= 2:
                    act.wait_ge(var_mm, k - 1)
                act.activation(ln_sq[:, k % 2, :], conv_c[:, k, :], ACT.Square).then_inc(xc_sq, 1)
            act.wait_ge(var_mm, KT)
            act.activation(ms, bank[NORM][:, :], ACT.Sqrt, bias=eps, scale=1.0 / D).then_inc(var_ms, 1)
            for k in range(KT):
                act.wait_ge(y_n, k + 1)
                act.activation(conv_c[:, k, :], conv_c[:, k, :], ACT.Silu, bias=p("ln_b", k),
                               scale=p("ln_g", k)).then_inc(y_s, 1)
                act.wait_ge(y_s, k + 1)
                act.activation(act_hi[:, k, :], conv_c[:, k, :], ACT.Copy).then_inc(a_hi_done, 1)

            def residual_units(first, count, stage, last=False):
                for u in range(count):
                    n = first + u
                    if n + 1 < UNITS:
                        split_weights(n + 1, (n + 1) % RING)
                    for j in range(2):
                        if stage is not None:
                            k = 2 * u + j
                            act.wait_ge(x_new, SQ[stage] - KT + k + 1)
                            xg_tile(stage, k)

            residual_units(FIRST["pw2"], KT // 2, "ffn0")

            def ffn(layer, next_stage):
                done = 0
                for c, count in enumerate(CHUNKS):
                    n0 = FIRST["in", layer, c]
                    f0 = layer * FT + sum(CHUNKS[:c])
                    t0 = sum(CHUNKS[:c])
                    if c == 0:
                        split_weights(n0 + 1, 1)
                        mean_square(1 if layer == 0 else 3)

                    def unit(i, j, split=True):
                        n, f, t = n0 + j + 2 * i, f0 + j + 2 * i, t0 + j + 2 * i
                        if split:
                            split_weights(n + 1, 1 - j)
                        for s in range(2):
                            act.wait_ge(u_done, 2 * f + s + 1)
                            act.wait_ge(a_lo_done, KT + f + 1)
                            at = layer * 2 * FT + s * FT
                            act.activation(ffn_t[:, 2 * j + s, :], ffn_u[:, 2 * j + s, FTAPS - 1:UP], ACT.Identity,
                                           bias=p("ffn_dw_b", at + t),
                                           scale=p("ffn_dw_w", (at + t) * FTAPS + FTAPS - 1)).then_inc(tap0, 1)
                        act.wait_ge(taps_done, 2 * f + 1)
                        act.activation(ffn_t[:, 2 * j, :], ffn_t[:, 2 * j, :], ACT.Silu).then_inc(silu_done, 1)
                        act.wait_ge(prod_done, f + 1)
                        act.activation(products(layer)[0][:, bass.ds(t - t0, 1), :], ffn_t[:, 2 * j + 1, :].rearrange("p (a b) -> p a b", a=1),
                                       ACT.Copy).then_inc(a_hi_done, 1)

                    if c == 0:
                        unit(0, 0, split=False)
                        unit(0, 1)
                        with act.Fori(1, count // 2) as i:
                            for j in range(2):
                                unit(i, j)
                    else:
                        with act.Fori(0, count // 2) as i:
                            for j in range(2):
                                unit(i, j)
                    residual_units(FIRST["out", layer, c], KT // 2, next_stage if c == 2 else None)

            ffn(0, "kv")

            for name in "vkq":
                for u in range(KT // 2):
                    n = FIRST[name] + u
                    split_weights(n + 1, (n + 1) % RING)
                    if name == "v":
                        if u == 0:
                            act.wait_ge(norm_mm, 3)
                            act.activation(rs_t_in, bank[NORM][:, 0:TB], ACT.Sqrt, bias=eps,
                                           scale=1.0 / D).then_inc(norm_ms, 1)
                            act.wait_ge(norm_rs, 3)
                        for b in range(TB):
                            act.wait_ge(tiles, TILE0 + 2 * n + b // 2 + 1)
                            act.activation(v_hi[:, b, u * 2 * P:(u + 1) * 2 * P],
                                           bank[2 * (n % RING) + b // 2][:, (b % 2) * 2 * P:(b % 2 + 1) * 2 * P],
                                           ACT.Copy, scale=rs_t[:, b:b + 1]).then_inc(v_hi_s, 1)
                if name != "v":
                    a = "kq".index(name)
                    act.wait_ge(kq_sum, a * KT + KT)
                    act.activation(stat_in[:, a].rearrange("p a b -> p (a b)"), stat[:, a].rearrange("p a b -> p (a b)"),
                                   ACT.Sqrt, bias=eps, scale=1.0 / HD).then_inc(kq_root, 1)
                if name == "k":
                    act.wait_ge(tiles, TILE0 + 2 * FIRST["q"])
                    for k in range(KT):
                        xg_tile("attn", k, square=False)

            with act.Fori(0, HEADS) as h:
                act.wait_ge(tr_done, 2 * h + 1)
                act.activation(kT_hi, bank[0][:, :], ACT.Copy, scale=p("k_norm_g")).then_inc(kT_h, 1)
                act.wait_ge(tr_done, 2 * h + 2)
                act.activation(qT_hi, bank[1][:, :], ACT.Copy, scale=gq8).then_inc(kT_h, 1)

                def exps(b):
                    for c in range(2):
                        act.wait_ge(m_done, 8 * h + 2 * b + c + 1)
                        act.activation(prob[:, b % 2, c, 0:(b + 1) * P], bank[2 + 2 * (b % 2) + c][:, 0:(b + 1) * P],
                                       ACT.Exp, bias=neg_max[:, 2 * b + c:2 * b + c + 1],
                                       accum_out=prob_sum[:, 2 * b + c:2 * b + c + 1]).then_inc(e_done, 1)

                def d_hi(b):
                    act.wait_ge(dt_done, 4 * h + b + 1)
                    act.activation(dT_hi[:, 0:b + 1, b * P:(b + 1) * P],
                                   bank[6][:, 0:(b + 1) * P].rearrange("p (a b) -> p a b", a=b + 1),
                                   ACT.Copy).then_inc(dT_h, 1)

                exps(0)
                exps(1)
                d_hi(0)
                exps(2)
                d_hi(1)
                exps(3)
                d_hi(2)
                d_hi(3)
                act.wait_ge(oT_done, h + 1)
                act.activation(xg_hi[:, bass.ds(h, 1), :], bank[0][:, :].rearrange("p (a b) -> p a b", a=1), ACT.Copy,
                               scale=gsub).then_inc(oT_h, 1)
            residual_units(FIRST["wo"], KT // 2, "ffn1")
            ffn(1, None)

        @block.vector
        def _(dve):
            own = Own(dve, dve_own)
            sub = ALU.subtract

            def split_weights(n, j):
                dve.wait_ge(w_hi_done, n + 1)
                dve.tensor_tensor(w_lo[:, j, :], w_raw[:, j, :], w_hi[:, j, :].bitcast(F32), sub).then_inc(w_lo_done, 1)

            def xg_lo_tile(stage, k):
                name, at = gains[stage] if stage in gains else ("attn_norm_g", 0)
                dve.wait_ge(xg_hi_done, XG[stage] + k + 1)
                dve.scalar_tensor_tensor(out=operand(stage)[1][:, k, :], in0=x[:, k, :], scalar=p(name, at + k),
                                         in1=operand(stage)[0][:, k, :].bitcast(F32), op0=ALU.mult, op1=sub).then_inc(xg_lo_done, 1)

            own.mark(dve.memset(ones[:, :], 1.0))
            own.mark(dve.memset(conv_u[:, :, 0:TAPS - 1], 0.0))
            n = own.mark(dve.memset(eps, EPS))
            own.wait(n)
            dve.sem_inc(banks_free, RING)
            dve.sem_inc(a_lo_done, 2)
            dve.sem_inc(sq_added, 2)
            dve.sem_inc(dve_const, 1)
            dve.wait_ge(par_in, 16)
            dve.wait_ge(lam_in_sem, 16)
            own.wait(own.mark(dve.tensor_tensor(lam_prod, lam_in[:, 0:2], lam_in[:, 2:4], ALU.mult)))
            dve.tensor_reduce(lam_sum, lam_prod, AX_X, ALU.add).then_inc(lam_summed, 1)
            own.mark(dve.tensor_scalar(gq8, p("q_norm_g"), HD ** -0.5, None, ALU.mult))
            own.mark(dve.tensor_scalar(gsub, p("subln_g"), 1.0 - LAM_INIT, None, ALU.mult))
            dve.wait_ge(lam_exped, 1)
            own.wait(own.mark(dve.tensor_tensor(neg_lam, lam_exp[:, 1:2], lam_exp[:, 0:1], sub)))
            own.wait(own.mark(dve.tensor_scalar(neg_lam, neg_lam, LAM_INIT, None, sub)))
            for k in range(KT):
                dve.wait_ge(x_in[k], 16)
                xg_lo_tile("conv", k)
                if k == 1:
                    split_weights(0, 0)

            def inverse_root(n):
                dve.wait_ge(norm_ms, n)
                dve.reciprocal(rs, ms).then_inc(norm_rs, 1)
                dve.wait_ge(norm_rs, n)

            inverse_root(1)
            PER = TAPS
            with own.loop(KT // 2, 2 * PER) as i:
                for j in range(2):
                    m = 2 * i + j
                    dve.wait_ge(tiles, TILE0 + 2 * m + 1)
                    a = own.mark(dve.tensor_tensor(conv_a[:, 0, :], bank[2 * j][:, :], rs, ALU.mult))
                    split_weights(m + 1, 1 - j)
                    dve.wait_ge(tiles, TILE0 + 2 * m + 2)
                    dve.tensor_tensor(conv_a[:, 1, :], bank[2 * j + 1][:, :], rs, ALU.mult).then_inc(c_g, 1)
                    own.wait(a)
                    dve.wait_ge(c_sig, m + 1)
                    dve.sem_inc(banks_free, 1)
                    dve.scalar_tensor_tensor(out=conv_u[:, j, TAPS - 1:CP], in0=conv_a[:, 0, :], scalar=p("pw1_b", m),
                                             in1=conv_a[:, 1, :], op0=ALU.add, op1=ALU.mult).then_inc(c_u, 1)
                    dve.wait_ge(c_u, m + 1)
                    last = [None, None]
                    c_tile = conv_c[:, bass.ds(m, 1), :].rearrange("p a b -> p (a b)")
                    chain = [conv_b, c_tile]
                    for t in range(1, TAPS):
                        which = t % 2
                        src = conv_u[:, j, t:t + SEQ]
                        w = p("dw_w", m * TAPS + t)
                        if t == 1:
                            last[1] = own.mark(dve.tensor_scalar(chain[1], src, w, None, ALU.mult))
                            continue
                        if t == 2:
                            dve.wait_ge(c_tap, m + 1)
                        if last[which] is not None:
                            own.wait(last[which])
                        last[which] = own.mark(dve.scalar_tensor_tensor(out=chain[which], in0=src, scalar=w,
                                                                        in1=chain[which], op0=ALU.mult, op1=ALU.add))
                    own.wait(last[0])
                    own.wait(last[1])
                    dve.tensor_tensor(c_tile, chain[1], chain[0], ALU.add).then_inc(c_done, 1)

            dve.wait_ge(mean_sb, 1)
            for k in range(KT):
                dve.tensor_tensor(conv_c[:, k, :], conv_c[:, k, :], ln_mean, sub).then_inc(xc_done, 1)
            dve.wait_ge(var_ms, 1)
            dve.reciprocal(rs, ms).then_inc(var_rs, 1)
            dve.wait_ge(var_rs, 1)
            dve.wait_ge(xc_done, KT)
            for k in range(KT + 1):
                if k < KT:
                    dve.tensor_tensor(conv_c[:, k, :], conv_c[:, k, :], rs, ALU.mult).then_inc(y_n, 1)
                if k >= 1:
                    dve.wait_ge(a_hi_done, k)
                    dve.tensor_tensor(act_lo[:, k - 1, :], conv_c[:, k - 1, :], act_hi[:, k - 1, :].bitcast(F32),
                                      sub).then_inc(a_lo_done, 1)

            def residual_units(first, stage, bias=None):
                for u in range(KT // 2):
                    n = first + u
                    for j in range(2):
                        k = 2 * u + j
                        dve.wait_ge(tiles, TILE0 + 2 * n + j + 1)
                        b = bank[2 * (n % RING) + j][:, :]
                        if bias is None:
                            new = dve.tensor_tensor(x[:, k, :], b, x[:, k, :], ALU.add)
                        else:
                            new = dve.scalar_tensor_tensor(out=x[:, k, :], in0=b, scalar=p(bias, k), in1=x[:, k, :],
                                                           op0=ALU.add, op1=ALU.add)
                        if stage is not None:
                            new.then_inc(x_new, 1)
                        else:
                            own.mark(new)
                        if j == 0 and n + 1 < UNITS:
                            split_weights(n + 1, (n + 1) % RING)
                        if stage not in (None, "out"):
                            xg_lo_tile(stage, k)
                    if stage is not None:
                        dve.wait_ge(x_new, (4 * KT if stage == "out" else SQ[stage]) - KT + k + 1)
                    else:
                        own.wait(own.count)
                    dve.sem_inc(banks_free, 1)

            residual_units(FIRST["pw2"], "ffn0", "pw2_b")

            def ffn(layer, next_stage):
                own.wait(own.mark(dve.memset(ffn_u[:, :, 0:FTAPS - 1], 0.0)))
                inverse_root(2 if layer == 0 else 4)
                for c, count in enumerate(CHUNKS):
                    n0 = FIRST["in", layer, c]
                    f0 = layer * FT + sum(CHUNKS[:c])
                    t0 = sum(CHUNKS[:c])
                    with own.loop(count // 2, 4) as i:
                        for j in range(2):
                            n, f, t = n0 + j + 2 * i, f0 + j + 2 * i, t0 + j + 2 * i
                            for s in range(2):
                                dve.wait_ge(tiles, TILE0 + 2 * n + s + 1)
                                u = ffn_u[:, 2 * j + s, :]
                                v = ffn_t[:, 2 * j + s, :]
                                w = (layer * 2 * FT + s * FT + t) * FTAPS
                                dve.tensor_tensor(u[:, FTAPS - 1:UP], bank[2 * j + s][:, :], rs, ALU.mult).then_inc(u_done, 1)
                                if s == 0:
                                    split_weights(n + 1, 1 - j)
                                dve.wait_ge(u_done, 2 * f + s + 1)
                                if s == 1:
                                    dve.sem_inc(banks_free, 1)
                                dve.wait_ge(tap0, 2 * f + s + 1)
                                own.wait(own.mark(dve.scalar_tensor_tensor(
                                    out=v, in0=u[:, 1:1 + SEQ], scalar=p("ffn_dw_w", w + 1), in1=v,
                                    op0=ALU.mult, op1=ALU.add)))
                                dve.scalar_tensor_tensor(out=v, in0=u[:, 0:SEQ], scalar=p("ffn_dw_w", w), in1=v,
                                                         op0=ALU.mult, op1=ALU.add).then_inc(taps_done, 1)
                            dve.wait_ge(taps_done, 2 * f + 2)
                            dve.wait_ge(silu_done, f + 1)
                            dve.tensor_tensor(v, v, ffn_t[:, 2 * j, :], ALU.mult).then_inc(prod_done, 1)
                            dve.wait_ge(a_hi_done, KT + f + 1)
                            hi, lo = products(layer)
                            dve.tensor_tensor(lo[:, bass.ds(t - t0, 1), :], v.rearrange("p (a b) -> p a b", a=1),
                                              hi[:, bass.ds(t - t0, 1), :].bitcast(F32), sub).then_inc(a_lo_done, 1)
                    residual_units(FIRST["out", layer, c], next_stage if c == 2 else None)

            ffn(0, "kv")
            for a, name in enumerate("vkq"):
                for u in range(KT // 2):
                    n = FIRST[name] + u
                    if a == 0 and u == 0:
                        dve.wait_ge(norm_ms, 3)
                        dve.reciprocal(rs_t, rs_t_in).then_inc(norm_rs, 1)
                        dve.wait_ge(norm_rs, 3)
                    for half_ in range(2):
                        dve.wait_ge(tiles, TILE0 + 2 * n + half_ + 1)
                        src = bank[2 * (n % RING) + half_]
                        for b in (2 * half_, 2 * half_ + 1):
                            from_ = src[:, (b % 2) * 2 * P:(b % 2 + 1) * 2 * P]
                            cols = slice(u * 2 * P, (u + 1) * 2 * P)
                            if name == "v":
                                dve.wait_ge(v_hi_s, TB * u + 2 * half_ + 2)
                                got = own.mark(dve.scalar_tensor_tensor(
                                    out=v_lo[:, b, cols], in0=from_, scalar=rs_t[:, b:b + 1],
                                    in1=v_hi[:, b, cols].bitcast(F32), op0=ALU.mult, op1=sub))
                            else:
                                to = (k_sb if name == "k" else q_sb)[:, b, cols]
                                got = own.mark(dve.tensor_scalar(to, from_, rs_t[:, b:b + 1], None, ALU.mult))
                        if half_ == 0:
                            split_weights(n + 1, (n + 1) % RING)
                        if name != "v":
                            t = (k_sb if name == "k" else q_sb)[:, 2 * half_:2 * half_ + 2, cols]
                            s2 = kq_sq[:, half_, :].rearrange("p (a b) -> p a b", a=2)
                            own.wait(got)
                            own.wait(own.mark(dve.tensor_tensor(s2, t, t, ALU.mult)))
                            dve.tensor_reduce(
                                stat[:, a - 1, 2 * half_:2 * half_ + 2, 4 * u:4 * u + 4],
                                kq_sq[:, half_, :].rearrange("p (a g d) -> p a g d", a=2, g=4),
                                AX_X, ALU.add).then_inc(kq_sum, 1)
                    own.wait(got)
                    dve.sem_inc(banks_free, 1)
                if name == "k":
                    for k in range(KT):
                        xg_lo_tile("attn", k)

            dve.wait_ge(kq_root, 2)
            dve.reciprocal(stat_rs[:, :].rearrange("p a b c -> p (a b c)"),
                           stat_in[:, :].rearrange("p a b c -> p (a b c)")).then_inc(kq_rs, 1)
            dve.wait_ge(kq_rs, 1)
            with own.loop(HEADS, 15) as h:
                for a, (to, of) in enumerate(((kn, k_sb), (qn, q_sb))):
                    r = stat_rs[:, a, :, bass.ds(2 * h, 2)]
                    for c in range(2):
                        ins = dve.tensor_tensor(
                            to[:, :, c * HD:(c + 1) * HD], of[:, :, bass.ds(h * P + c * HD, HD)],
                            stat_rs[:, a, :, bass.ds(2 * h + c, 1)].broadcast_to([P, TB, HD]), ALU.mult)
                        ins.then_inc(n_done, 1)
                for s, (hi, lo, g) in enumerate(((kT_hi, kT_lo, p("k_norm_g")), (qT_hi, qT_lo, gq8))):
                    dve.wait_ge(kT_h, 2 * h + s + 1)
                    dve.scalar_tensor_tensor(out=lo, in0=bank[s][:, :], scalar=g, in1=hi.bitcast(F32),
                                             op0=ALU.mult, op1=sub).then_inc(kT_l, 1)

                def maxima(b):
                    for c in range(2):
                        dve.wait_ge(s_done, 8 * h + 2 * b + c + 1)
                        dve.tensor_reduce(neg_max[:, 2 * b + c:2 * b + c + 1], bank[2 + 2 * (b % 2) + c][:, 0:(b + 1) * P],
                                          AX_X, ALU.max, negate=True).then_inc(m_done, 1)

                def differ(b):
                    w = slice(0, (b + 1) * P)
                    dve.wait_ge(e_done, 8 * h + 2 * b + 2)
                    own.wait(own.mark(dve.reciprocal(inv[:, 2 * b:2 * b + 2], prob_sum[:, 2 * b:2 * b + 2])))
                    own.wait(own.mark(dve.tensor_scalar(lam_inv[:, b:b + 1], inv[:, 2 * b + 1:2 * b + 2], neg_lam, None,
                                                        ALU.mult)))
                    own.wait(own.mark(dve.tensor_scalar(prob[:, b % 2, 1, w], prob[:, b % 2, 1, w], lam_inv[:, b:b + 1],
                                                        None, ALU.mult)))
                    dve.scalar_tensor_tensor(out=prob[:, b % 2, 0, w], in0=prob[:, b % 2, 0, w],
                                             scalar=inv[:, 2 * b:2 * b + 1], in1=prob[:, b % 2, 1, w],
                                             op0=ALU.mult, op1=ALU.add).then_inc(d_done, 1)

                def d_lo(b):
                    dve.wait_ge(dT_h, 4 * h + b + 1)
                    dve.tensor_tensor(dT_lo[:, 0:b + 1, b * P:(b + 1) * P],
                                      bank[6][:, 0:(b + 1) * P].rearrange("p (a b) -> p a b", a=b + 1),
                                      dT_hi[:, 0:b + 1, b * P:(b + 1) * P].bitcast(F32), sub).then_inc(dT_l, 1)

                maxima(0)
                maxima(1)
                differ(0)
                d_lo(0)
                maxima(2)
                differ(1)
                d_lo(1)
                maxima(3)
                differ(2)
                d_lo(2)
                differ(3)
                d_lo(3)
                dve.wait_ge(o_done, h + 1)
                own.wait(own.mark(dve.tensor_copy(o_sb.rearrange("p a b -> p (a b)"), bank[7][:, :])))
                own.wait(own.mark(dve.tensor_tensor(o_sq, o_sb, o_sb, ALU.mult)))
                own.wait(own.mark(dve.tensor_reduce(o_ms, o_sq, AX_X, ALU.add)))
                dve.tensor_scalar(o_in, o_ms, 1.0 / VD, EPS, ALU.mult, ALU.add).then_inc(o_sum, 1)
                dve.wait_ge(o_rs_s, h + 1)
                for b in range(TB):
                    dve.tensor_scalar(o_sb[:, b, :], o_sb[:, b, :], o_rs[:, b:b + 1], None, ALU.mult).then_inc(on_done, 1)
                dve.wait_ge(oT_h, h + 1)
                dve.scalar_tensor_tensor(out=xg_lo[:, bass.ds(h, 1), :], in0=bank[0][:, :].rearrange("p (a b) -> p a b", a=1),
                                         scalar=gsub, in1=xg_hi[:, bass.ds(h, 1), :].bitcast(F32),
                                         op0=ALU.mult, op1=sub).then_inc(oT_l, 1)
            residual_units(FIRST["wo"], "ffn1")
            ffn(1, "out")

        @block.tensor
        def _(pe):
            def weights(w, j, tiles_k, k, m):
                return w[:, j, (k * 2 + m) * P:(k * 2 + m + 1) * P]

            def passes(out, j, m, k, hi, lo, count):
                for s, (w, v) in enumerate(((w_hi, hi), (w_hi, lo), (w_lo, hi))):
                    got = pe.matmul(out, weights(w, j, count, k, m), v[:, k, :], start=(k == 0 and s == 0),
                                    stop=(k == count - 1 and s == 2), skip_group_check=True)
                return got

            def begin(n):
                pe.wait_ge(w_lo_done, n + 1)
                pe.wait_ge(banks_free, n + 1)

            def unit(n, j, hi, lo, count, late=0, ready=None, middle=None):
                begin(n)
                early = count - late
                for m in range(2):
                    for k in range(early):
                        if ready and m == 0:
                            ready(k)
                        got = passes(bank[2 * j + m][:, :], j, m, k, hi, lo, count)
                    if not late:
                        got.then_inc(tiles, 1)
                for m in range(2):
                    for k in range(early, count):
                        if ready and m == 0:
                            ready(k)
                        got = passes(bank[2 * j + m][:, :], j, m, k, hi, lo, count)
                    if late:
                        got.then_inc(tiles, 1)
                    if middle and m == 0:
                        middle()

            def square_sum(stage_n):
                pe.wait_ge(sq_added, 2 + KT * (stage_n + 1))
                pe.matmul(bank[NORM][:, :], ones[:, :], sq_sum, start=True, stop=True).then_inc(norm_mm, 1)

            def xg_ready(stage):
                return lambda k: pe.wait_ge(xg_lo_done, XG[stage] + k + 1)

            pe.wait_ge(dve_const, 1)
            pe.wait_ge(const_ready, 4)
            pe.sem_inc(tiles, TILE0)
            unit(0, 0, xg_hi, xg_lo, KT, 4, xg_ready("conv"), lambda: square_sum(0))
            unit(1, 1, xg_hi, xg_lo, KT)
            with pe.Fori(1, KT // 2) as i:
                for j in range(2):
                    unit(2 * i + j, j, xg_hi, xg_lo, KT)
            pe.wait_ge(c_added, KT)
            pe.matmul(bank[NORM][:, :], ones[:, :], ln_sum, start=True, stop=True).then_inc(mean_mm, 1)
            pe.wait_ge(mean_sb, 1)
            for k in range(KT):
                pe.wait_ge(xc_sq, k + 1)
                pe.matmul(bank[NORM][:, :], ones[:, :], ln_sq[:, k % 2, :], start=k == 0, stop=k == KT - 1).then_inc(var_mm, 1)

            def residual_units(first, hi, lo, count, late, ready):
                unit(first, 0, hi, lo, count, late, ready)
                unit(first + 1, 1, hi, lo, count)
                unit(first + 2, 0, hi, lo, count)
                unit(first + 3, 1, hi, lo, count)

            residual_units(FIRST["pw2"], act_hi, act_lo, KT, 2, lambda k: pe.wait_ge(a_lo_done, 2 + k + 1))

            def ffn(layer):
                hi, lo = operand(f"ffn{layer}")
                for c, count in enumerate(CHUNKS):
                    n0 = FIRST["in", layer, c]
                    i0 = 0
                    if c == 0:
                        unit(n0, 0, hi, lo, KT, 2, xg_ready(f"ffn{layer}"), lambda: square_sum(1 if layer == 0 else 3))
                        unit(n0 + 1, 1, hi, lo, KT)
                        i0 = 1
                    with pe.Fori(i0, count // 2) as i:
                        for j in range(2):
                            unit(n0 + 2 * i + j, j, hi, lo, KT)
                    a0 = 2 + KT + layer * FT + sum(CHUNKS[:c])
                    residual_units(FIRST["out", layer, c], *products(layer), count, 2, lambda k: pe.wait_ge(a_lo_done, a0 + k + 1))

            ffn(0)

            for name in "vkq":
                for u in range(KT // 2):
                    n = FIRST[name] + u
                    j = n % RING
                    begin(n)
                    for b in range(TB):
                        out = bank[2 * j + b // 2][:, (b % 2) * 2 * P:(b % 2 + 1) * 2 * P]
                        for k in range(KT):
                            if u == 0 and b == 0 and name != "k":
                                xg_ready("kv" if name == "v" else "attn")(k)
                            for s, (v, w) in enumerate(((xg_hi, w_hi), (xg_hi, w_lo), (xg_lo, w_hi))):
                                got = pe.matmul(out, v[:, k, b * P:(b + 1) * P], w[:, j, k * 2 * P:(k + 1) * 2 * P],
                                                start=(k == 0 and s == 0), stop=(k == KT - 1 and s == 2),
                                                skip_group_check=True)
                        if b % 2:
                            got.then_inc(tiles, 1)
                        if name == "v" and u == 0 and b == 1:
                            pe.wait_ge(sq_added, 2 + 3 * KT)
                            for t in range(TB):
                                last = pe.matmul(bank[NORM][:, t:t + 1], sq_sum[:, t * P:(t + 1) * P], ones[:, 0:1],
                                                 start=True, stop=True, skip_group_check=True)
                            last.then_inc(norm_mm, 1)

            with pe.Fori(0, HEADS) as h:
                for s, v in enumerate((kn, qn)):
                    pe.wait_ge(n_done, 4 * h + 2 * s + 2)
                    for b in range(TB):
                        got = pe.transpose(bank[s][:, b * P:(b + 1) * P], v[:, b, :], ident[:, :])
                    got.then_inc(tr_done, 1)

                def scores(b):
                    for c in range(2):
                        if b >= 2:
                            pe.wait_ge(e_done, 8 * h + 2 * (b - 2) + c + 1)
                        out = bank[2 + 2 * (b % 2) + c]
                        rows = slice(c * HD, (c + 1) * HD)
                        qs = slice(b * P, (b + 1) * P)
                        for s, (q, k) in enumerate(((qT_hi, kT_hi), (qT_hi, kT_lo), (qT_lo, kT_hi))):
                            pe.matmul(out[:, 0:(b + 1) * P], q[rows, qs], k[rows, 0:(b + 1) * P],
                                      start=s == 0, stop=False, skip_group_check=True)
                        pe.matmul(out[:, qs], ident16[:, :], mask16[:, :], start=False, stop=True,
                                  skip_group_check=True).then_inc(s_done, 1)

                def turn(b):
                    pe.wait_ge(d_done, 4 * h + b + 1)
                    if b >= 1:
                        pe.wait_ge(dT_l, 4 * h + b)
                    for k in range(b + 1):
                        got = pe.transpose(bank[6][:, k * P:(k + 1) * P], prob[:, b % 2, 0, k * P:(k + 1) * P], ident[:, :])
                    got.then_inc(dt_done, 1)

                pe.wait_ge(kT_l, 2 * h + 2)
                scores(0)
                scores(1)
                turn(0)
                scores(2)
                turn(1)
                scores(3)
                turn(2)
                turn(3)
                for b in range(TB):
                    pe.wait_ge(dT_l, 4 * h + b + 1)
                    for k in range(b + 1):
                        for s, (d, v) in enumerate(((dT_hi, v_hi), (dT_hi, v_lo), (dT_lo, v_hi))):
                            got = pe.matmul(bank[7][:, b * VD:(b + 1) * VD], d[:, k, b * P:(b + 1) * P],
                                            v[:, k, bass.ds(h * VD, VD)], start=(k == 0 and s == 0),
                                            stop=(k == b and s == 2), skip_group_check=True)
                got.then_inc(o_done, 1)
                pe.wait_ge(on_done, 4 * h + 4)
                for b in range(TB):
                    got = pe.transpose(bank[0][:, b * P:(b + 1) * P], o_sb[:, b, :], ident[:, :])
                got.then_inc(oT_done, 1)
                pe.wait_ge(oT_l, h + 1)
            residual_units(FIRST["wo"], xg_hi, xg_lo, KT, 0, None)
            ffn(1)


def column_tiles(v):
    return v.reshape(-1, P).T


def unit_block(w, rows, columns):
    w = w[rows[0] * P:(rows[0] + rows[1]) * P]
    w = np.concatenate([w[:, c * P:(c + 1) * P] for c in columns], axis=1)
    return w.reshape(rows[1], P, 2 * P).transpose(1, 0, 2).reshape(P, rows[1] * 2 * P)


def stream_of(i):
    blocks = []
    pairs = [(2 * u, 2 * u + 1) for u in range(KT // 2)]

    def ffn(layer):
        done = 0
        for tiles in CHUNKS:
            blocks.extend(unit_block(i["ffn_w_in"][layer], (0, KT), (done + t, FT + done + t)) for t in range(tiles))
            blocks.extend(unit_block(i["ffn_w_out"][layer], (done, tiles), c) for c in pairs)
            done += tiles

    blocks.extend(unit_block(i["conv_pw1_w"][0], (0, KT), (t, KT + t)) for t in range(KT))
    blocks.extend(unit_block(i["conv_pw2_w"][0], (0, KT), c) for c in pairs)
    ffn(0)
    for w in (i["w_v"], i["w_k"], i["w_q"][0], i["w_o"][0]):
        blocks.extend(unit_block(w, (0, KT), c) for c in pairs)
    ffn(1)
    return np.ascontiguousarray(np.concatenate(blocks, axis=1))


def kernel(**inputs):
    import concourse.bacc as _bacc
    from concourse.bass_utils import run_bass_kernel_spmd as _run

    i = {name: np.asarray(v) for name, v in inputs.items()}
    twice = lambda v: np.concatenate([v, v]).reshape(P, 1)
    params = np.concatenate([
        column_tiles(i["conv_norm_g"]), column_tiles(i["conv_pw1_b"]),
        i["conv_dw_w"][0].reshape(TAPS, KT, P).transpose(2, 1, 0).reshape(P, KT * TAPS),
        column_tiles(i["conv_dw_b"]), column_tiles(i["conv_ln_g"]), column_tiles(i["conv_ln_b"]),
        column_tiles(i["conv_pw2_b"]), column_tiles(i["kv_norm_g"]), column_tiles(i["attn_norm_g"]),
        column_tiles(i["ffn_norm_g"]),
        i["ffn_dw_w"].reshape(2, FTAPS, 2 * FT, P).transpose(3, 0, 2, 1).reshape(P, 2 * 2 * FT * FTAPS),
        column_tiles(i["ffn_dw_b"]), twice(i["k_norm_g"]), twice(i["q_norm_g"][0]), i["subln_g"][0].reshape(P, 1),
    ], axis=1)
    lambdas = np.stack([i["lambda_q1"][0], i["lambda_q2"][0], i["lambda_k1"][0], i["lambda_k2"][0]])
    arrays = {
        "x_t": np.ascontiguousarray(i["x"][0].T),
        "stream": stream_of(i),
        "params": np.ascontiguousarray(params),
        "lambdas": np.ascontiguousarray(np.broadcast_to(lambdas, (P, 4, HD))),
    }
    nc = _bacc.Bacc("TRN2", target_bir_lowering=False, num_devices=1)
    args = [nc.dram_tensor(n, a.shape, F32, kind="ExternalInput").ap() for n, a in arrays.items()]
    out = nc.dram_tensor("out_t", (D, SEQ), F32, kind="ExternalOutput").ap()
    trunk(nc, *args, out)
    got = _run(nc, [arrays], core_ids=[0]).results[0]["out_t"]
    return np.ascontiguousarray(got.T).reshape(1, SEQ, D)
```

```python
import math
from contextlib import ExitStack, contextmanager

import numpy as np

import concourse.bass as bass
from concourse import mybir

F32 = mybir.dt.float32
F32R = mybir.dt.float32r
BF16 = mybir.dt.bfloat16
ALU = mybir.AluOpType
ACT = mybir.ActivationFunctionType
AX_X = mybir.AxisListType.X

P = 128
D = 1024
SEQ = 512
KT = D // P
TB = SEQ // P
TAPS = 31
D_FF = 2816
FT = D_FF // P
FTAPS = 3
HEADS = 8
HD = 64
VD = 2 * HD
EPS = 1e-6
NEG = -1e30
LAM_INIT = 0.8 - 0.6 * math.exp(-0.3)
RING = 2
SLOT = KT * 2 * P
TILE0 = 2
GROUPS = HEADS // 2
CHUNKS = [KT, KT, FT - 2 * KT]

PARAM_WIDTHS = [
    ("conv_norm_g", KT), ("pw1_b", 2 * KT), ("dw_w", KT * TAPS), ("dw_b", KT), ("ln_g", KT), ("ln_b", KT),
    ("pw2_b", KT), ("kv_norm_g", KT), ("attn_norm_g", KT), ("ffn_norm_g", 2 * KT), ("ffn_dw_w", 2 * 2 * FT * FTAPS),
    ("ffn_dw_b", 2 * 2 * FT), ("k_norm_g", 1), ("q_norm_g", 1), ("subln_g", 1),
]
PARAM_AT = {}
N_PARAMS = 0
for _name, _width in PARAM_WIDTHS:
    PARAM_AT[_name] = N_PARAMS
    N_PARAMS += _width


def unit_plan():
    first, widths = {}, []

    def phase(name, count, width=SLOT):
        first[name] = len(widths)
        widths.extend([width] * count)

    def ffn(layer):
        for c, tiles in enumerate(CHUNKS):
            phase(("in", layer, c), tiles)
            phase(("out", layer, c), KT // 2, tiles * 2 * P)

    phase("pw1", KT)
    phase("pw2", KT // 2)
    ffn(0)
    phase("kqv", GROUPS * 3)
    phase("wo", KT // 2)
    ffn(1)
    starts = [sum(widths[:n]) for n in range(len(widths) + 1)]
    return first, widths, starts


FIRST, WIDTHS, STARTS = unit_plan()
UNITS = len(WIDTHS)


SETS = [[3], [2, 0], [1]]
ORDER = [b for blocks in SETS for b in blocks]
PLACE = {b: ORDER.index(b) for b in ORDER}
SET_OF = {b: n for n, blocks in enumerate(SETS) for b in blocks}
COLUMN = {3: 0, 2: 0, 0: 3 * P, 1: 0}
TRI = {b: b * (b + 1) // 2 * P for b in ORDER}


def component(h, n, c):
    return 8 * h + 2 * PLACE[SETS[n][0]] + (c + 1) * len(SETS[n])


SLOTS = [["turn K"], ["turn C"], [], ["turn Q"], ["output"], ["score A"], ["norm output"], ["score B"],
         ["turn output"], ["turn A"], ["score C"], ["turn B"]]
LATE = ("turn C", "output", "norm output", "turn output")
LETTER = {"A": 0, "B": 1, "C": 2}


def attention_schedule(dense, step):
    for g in range(GROUPS + 1):
        for q in range(24):
            dense(g, q)
            if g >= 1:
                h = 2 * (g - 1) + q // 12
                for name in SLOTS[q % 12]:
                    if name not in LATE:
                        step(h, name)
                    elif h:
                        step(h - 1, name)
    for name in LATE:
        step(HEADS - 1, name)


class Own:

    def __init__(self, engine, semaphore):
        self.engine, self.semaphore, self.base, self.count = engine, semaphore, 0, 0

    def mark(self, instruction):
        instruction.then_inc(self.semaphore, 1)
        self.count += 1
        return self.count

    def wait(self, count):
        self.engine.wait_ge(self.semaphore, self.base + count)

    @contextmanager
    def loop(self, times, each):
        before = self.base + self.count
        with self.engine.Fori(0, times) as i:
            self.base, self.count = before + each * i, 0
            yield i
            assert self.count == each, (self.count, each)
        self.base, self.count = before + each * times, 0


def trunk(nc, x_t, stream, params, lambdas, out_t):
    with ExitStack() as ctx:
        def sb(name, shape, dtype=F32):
            return ctx.enter_context(nc.sbuf_tensor(name, shape, dtype))

        def sem(name):
            return ctx.enter_context(nc.semaphore(name))

        top = -(-nc.sbuf_base // 64) * 64

        def put(name, at, shape, dtype=F32):
            size = 2 if dtype == BF16 else 4
            end = at + -(-math.prod(shape[1:]) * size // 64) * 64
            return nc.alloc_sbuf_tensor_at(name, shape, dtype, offset=at)[(slice(None),) * len(shape)], end

        x, at = put("x", top, [P, KT, SEQ])
        xg_hi, at = put("xg_hi", at, [P, KT, SEQ], F32R)
        xg_lo, at = put("xg_lo", at, [P, KT, SEQ], F32R)
        w_raw, at = put("w_raw", at, [P, RING, SLOT])
        w_hi, at = put("w_hi", at, [P, RING, SLOT], F32R)
        w_lo, at = put("w_lo", at, [P, RING, SLOT], F32R)
        par, at = put("par", at, [P, N_PARAMS])
        ident, at = put("ident", at, [P, P])
        ones, at = put("ones", at, [P, P])
        ident16, at = put("ident16", at, [P, P], BF16)
        mask16, at = put("mask16", at, [P, P], BF16)
        small, at = put("small", at, [P, 96])
        act_hi, at = put("act_hi", at, [P, KT, SEQ], F32R)
        act_lo, area = put("act_lo", at, [P, KT, SEQ], F32R)
        eps = small[:, 0:1]
        gq8 = small[:, 1:2]
        gsub = small[:, 2:3]
        neg_lam = small[:, 3:4]
        lam_sum = small[:, 4:6]
        lam_exp = small[:, 6:8]
        rs_t = small[:, 8:12]
        rs_t_in = small[:, 12:16]
        neg_max = small[:, 16:24]
        prob_sum = small[:, 24:32]
        inv = small[:, 32:40]
        lam_inv = small[:, 40:44]
        o_ms = small[:, 44:48]
        o_in = small[:, 48:52]
        o_rs = small[:, 52:56]
        half = small[:, 56:57]
        stat = small[:, 60:76]
        stat_in = small[:, 76:92]

        sq, at = put("sq", area, [P, 2, SEQ])
        sq_sum, at = put("sq_sum", at, [P, SEQ])
        rs, at = put("rs", at, [P, SEQ])
        ms, own_area = put("ms", at, [P, SEQ])
        UP = SEQ + FTAPS - 1
        ffn_u, at = put("ffn_u", own_area, [P, 4, UP])
        ffn_t, at = put("ffn_t", at, [P, 4, SEQ])
        CP = SEQ + TAPS - 1
        conv_u, at = put("conv_u", own_area, [P, 2, CP])
        conv_a, at = put("conv_a", at, [P, 2, SEQ])
        conv_b, at = put("conv_b", at, [P, SEQ])
        conv_c, at = put("conv_c", at, [P, KT, SEQ])
        ln_mean, at = put("ln_mean", at, [P, SEQ])
        ln_sq, at = put("ln_sq", at, [P, 2, SEQ])
        ln_sum, at = put("ln_sum", at, [P, SEQ])
        lam_in, at = put("lam_in", at, [P, 4, HD])
        lam_prod, at = put("lam_prod", at, [P, 2, HD])
        v_hi, at = put("v_hi", area, [P, 2, TB, 2 * VD], F32R)
        v_lo, at = put("v_lo", at, [P, 2, TB, 2 * VD], F32R)
        k_sb, at = put("k_sb", at, [P, 2, TB, 2 * P])
        q_sb, at = put("q_sb", at, [P, 2, TB, 2 * P])
        kq_sq, at = put("kq_sq", at, [P, TB, 2 * P])
        kT_hi, at = put("kT_hi", at, [P, SEQ], F32R)
        kT_lo, at = put("kT_lo", at, [P, SEQ], F32R)
        qT_hi, at = put("qT_hi", at, [P, SEQ], F32R)
        qT_lo, at = put("qT_lo", at, [P, SEQ], F32R)
        dT_hi, at = put("dT_hi", at, [P, 10 * P], F32R)
        dT_lo, at = put("dT_lo", at, [P, 10 * P], F32R)
        prob, at = put("prob", at, [P, 2, 2, SEQ])
        o_sb, at = put("o_sb", at, [P, TB, VD])

        bank = [ctx.enter_context(nc.psum_tensor(f"bank{n}", [P, SEQ], F32)) for n in range(8)]
        NORM = 7

        par_in = sem("par_in")
        lam_in_sem = sem("lam_in")
        x_in = [sem(f"x_in{n}") for n in range(KT)]
        w_in = [sem(f"w_in{n}") for n in range(RING)]
        w_hi_done = sem("w_hi_done")
        w_hi_part = sem("w_hi_part")
        w_lo_done = sem("w_lo_done")
        tiles = sem("tiles")
        banks_free = sem("banks_free")
        const_ready = sem("const_ready")
        lam_summed = sem("lam_summed")
        lam_exped = sem("lam_exped")
        dve_own = sem("dve_own")
        pool_own = sem("pool_own")
        dve_const = sem("dve_const")
        x_new = sem("x_new")
        xg_hi_done = sem("xg_hi_done")
        xg_lo_done = sem("xg_lo_done")
        sq_done = sem("sq_done")
        sq_added = sem("sq_added")
        norm_mm = sem("norm_mm")
        norm_ms = sem("norm_ms")
        norm_rs = sem("norm_rs")
        u_done = sem("u_done")
        tap0 = sem("tap0")
        taps_done = sem("taps_done")
        silu_done = sem("silu_done")
        prod_done = sem("prod_done")
        a_hi_done = sem("a_hi_done")
        a_lo_done = sem("a_lo_done")
        c_g = sem("c_g")
        c_sig = sem("c_sig")
        c_u = sem("c_u")
        c_tap = sem("c_tap")
        c_done = sem("c_done")
        c_added = sem("c_added")
        mean_mm = sem("mean_mm")
        mean_sb = sem("mean_sb")
        xc_done = sem("xc_done")
        xc_sq = sem("xc_sq")
        var_mm = sem("var_mm")
        var_ms = sem("var_ms")
        var_rs = sem("var_rs")
        y_n = sem("y_n")
        y_s = sem("y_s")
        xb = sem("xb")
        kqv_half = sem("kqv_half")
        v_hi_s = sem("v_hi_s")
        kq_squared = sem("kq_squared")
        kq_summed = sem("kq_summed")
        kq_normed = sem("kq_normed")
        turned = sem("turned")
        turned_hi = sem("turned_hi")
        turned_lo = sem("turned_lo")
        s_done = sem("s_done")
        m_done = sem("m_done")
        e_done = sem("e_done")
        d_done = sem("d_done")
        dt_done = sem("dt_done")
        dT_h = sem("dT_h")
        dT_l = sem("dT_l")
        o_done = sem("o_done")
        o_squared = sem("o_squared")
        o_root = sem("o_root")
        o_normed = sem("o_normed")
        oT_done = sem("oT_done")
        oT_h = sem("oT_h")
        oT_l = sem("oT_l")
        out_s = sem("out_s")

        def p(name, n=0, width=1):
            at = PARAM_AT[name] + n
            return par[:, bass.ds(at, width)]

        stages = ["conv", "ffn0", "kv", "ffn1"]
        gains = {"conv": ("conv_norm_g", 0), "ffn0": ("ffn_norm_g", 0), "kqv": None, "ffn1": ("ffn_norm_g", KT)}
        row_gain = {FIRST["kqv"] + 3 * g + u: ("kv_norm_g", "attn_norm_g", "kv_norm_g")[u]
                    for g in range(GROUPS) for u in range(3)}
        XG = {"conv": 0, "ffn0": KT, "kqv": 2 * KT, "ffn1": 3 * KT}
        SQ = XG

        block = ctx.enter_context(nc.Block())

        @block.sync
        def _(sp):
            sp.dma_start(par[:, :], params).then_inc(par_in, 16)
            sp.dma_start(lam_in, lambdas).then_inc(lam_in_sem, 16)
            for k in range(KT):
                sp.dma_start(x[:, k, :], x_t[k * P:(k + 1) * P, :]).then_inc(x_in[k], 16)
                if k < RING:
                    sp.dma_start(w_raw[:, k, :], stream[:, STARTS[k]:STARTS[k + 1]]).then_inc(w_in[k], 16)
            n = RING
            while n < UNITS:
                width = WIDTHS[n]
                count = 1
                while n + count < UNITS and WIDTHS[n + count] == width:
                    count += 1
                assert n % RING == 0 and count % RING == 0
                with sp.Fori(0, count // RING) as i:
                    for j in range(RING):
                        sp.wait_ge(w_lo_done, n + j - RING + 1 + RING * i)
                        sp.dma_start(w_raw[:, j, 0:width],
                                     stream[:, bass.ds(STARTS[n] + j * width + RING * width * i, width)]
                                     ).then_inc(w_in[j], 16)
                n += count
            for k in range(KT):
                sp.wait_ge(x_new, 3 * KT + k + 1)
                sp.dma_start(out_t[k * P:(k + 1) * P, :], x[:, k, :]).then_inc(out_s, 16)
            sp.wait_ge(out_s, 16 * KT)

        @block.gpsimd
        def _(pool):
            own = Own(pool, pool_own)
            own.mark(pool.memset(ident[:, :], 0.0))
            own.mark(pool.memset(ident16[:, :], 0.0))
            n = own.mark(pool.memset(mask16[:, :], 0.0))
            own.wait(n)
            pool.affine_select(out=ident[:, :], in_=ident[:, :], compare_op=ALU.not_equal, fill=1.0, base=0,
                               pattern=[[-1, P]], channel_multiplier=1).then_inc(const_ready, 1)
            pool.affine_select(out=ident16[:, :], in_=ident16[:, :], compare_op=ALU.not_equal, fill=1.0, base=0,
                               pattern=[[-1, P]], channel_multiplier=1).then_inc(const_ready, 1)
            pool.affine_select(out=mask16[:, :], in_=mask16[:, :], compare_op=ALU.is_ge, fill=NEG, base=0,
                               pattern=[[-1, P]], channel_multiplier=1).then_inc(const_ready, 1)
            pool.memset(half[:, :], -0.5).then_inc(const_ready, 1)
            pool.wait_ge(const_ready, 4)

            def sum_squares(stage):
                at = SQ[stage]
                for k in range(KT):
                    pool.wait_ge(sq_done, at + k + 1)
                    if k == 0:
                        pool.tensor_copy(sq_sum, sq[:, k % 2, :]).then_inc(sq_added, 1)
                    else:
                        pool.wait_ge(sq_added, 2 + at + k)
                        pool.tensor_tensor(sq_sum, sq_sum, sq[:, k % 2, :], ALU.add).then_inc(sq_added, 1)

            def power(out, in_, shape):
                return pool.tensor_tensor(out, in_, half.broadcast_to(shape), ALU.pow)

            sum_squares("conv")
            for k in range(KT):
                pool.wait_ge(c_done, k + 1)
                if k == 0:
                    pool.tensor_copy(ln_sum, conv_c[:, k, :]).then_inc(c_added, 1)
                else:
                    pool.wait_ge(c_added, k)
                    pool.tensor_tensor(ln_sum, ln_sum, conv_c[:, k, :], ALU.add).then_inc(c_added, 1)
            sum_squares("ffn0")
            sum_squares("kqv")

            def dense(g, q):
                if g == GROUPS or q % 2 == 0:
                    return
                q //= 2
                u, part = divmod(q, 4)
                if u < 2 and part % 2 == 1:
                    kq = (k_sb, q_sb)[u][:, g % 2, part - 1:part + 1, :]
                    pool.wait_ge(kqv_half, 6 * g + 2 * u + part // 2 + 1)
                    if (g, u) > (0, 0):
                        pool.wait_ge(kq_summed, 2 * g + u)
                    pool.tensor_tensor(kq_sq[:, part - 1:part + 1, :], kq, kq, ALU.mult).then_inc(kq_squared, 1)
                if q in (6, 10):
                    u = q // 8
                    pool.wait_ge(kq_summed, 2 * g + u + 1)
                    own.wait(own.mark(pool.tensor_scalar(stat_in, stat, 1.0 / HD, EPS, ALU.mult, ALU.add)))
                    own.wait(own.mark(power(stat_in, stat_in, [P, 4 * TB])))
                    kq = (k_sb, q_sb)[u][:, g % 2, :, :].rearrange("p b (c d) -> p (b c) d", c=4)
                    pool.tensor_tensor(kq, kq, stat_in.rearrange("p (a b) -> p a b", b=1).broadcast_to([P, 4 * TB, HD]),
                                       ALU.mult).then_inc(kq_normed, 1)

            def step(h, name):
                if name == "output":
                    pool.wait_ge(o_squared, h + 1)
                    own.wait(own.mark(pool.tensor_scalar(o_in, o_ms, 1.0 / VD, EPS, ALU.mult, ALU.add)))
                    power(o_rs, o_in, [P, TB]).then_inc(o_root, 1)

            attention_schedule(dense, step)
            sum_squares("ffn1")

        @block.scalar
        def _(act):
            def split_weights(n, j):
                act.wait_ge(w_in[j], (n - j) * (16 // RING) + 16)
                act.wait_ge(tiles, TILE0 + 2 * n - 2)
                act.activation(w_hi[:, j, :], w_raw[:, j, :], ACT.Copy).then_inc(w_hi_done, 1)

            def split_gained(n, parts):
                j = n % RING
                if 0 in parts:
                    act.wait_ge(w_in[j], (n - j) * (16 // RING) + 16)
                    act.wait_ge(tiles, TILE0 + 2 * n - 2)
                for k in (2 * part + i for part in parts for i in range(2)):
                    cols = slice(k * 2 * P, (k + 1) * 2 * P)
                    got = act.activation(w_hi[:, j, cols], w_raw[:, j, cols], ACT.Copy, scale=p(row_gain[n], k))
                    if k % 2:
                        got.then_inc(w_hi_part, 1)

            def xg_tile(stage, k, square=True):
                scale = p(gains[stage][0], gains[stage][1] + k) if gains[stage] else 1.0
                act.activation(xg_hi[:, k, :], x[:, k, :], ACT.Copy, scale=scale).then_inc(xg_hi_done, 1)
                if square:
                    act.wait_ge(sq_added, SQ[stage] + k + 1)
                    act.activation(sq[:, k % 2, :], x[:, k, :], ACT.Square).then_inc(sq_done, 1)

            def mean_square(stage_n):
                act.wait_ge(norm_mm, stage_n + 1)
                act.activation(ms, bank[NORM][:, :], ACT.Sqrt, bias=eps, scale=1.0 / D).then_inc(norm_ms, 1)

            act.wait_ge(par_in, 16)
            act.wait_ge(dve_const, 1)
            act.wait_ge(lam_summed, 1)
            act.activation(lam_exp, lam_sum, ACT.Exp).then_inc(lam_exped, 1)
            for k in range(KT):
                act.wait_ge(x_in[k], 16)
                xg_tile("conv", k)
                if k == 1:
                    split_weights(0, 0)
            mean_square(0)

            def conv_unit(m, j, n):
                split_weights(n + 1, 1 - j)
                act.wait_ge(c_g, m + 1)
                act.activation(conv_a[:, 1, :], conv_a[:, 1, :], ACT.Sigmoid, bias=p("pw1_b", KT + m)).then_inc(c_sig, 1)
                act.wait_ge(c_u, m + 1)
                act.activation(conv_b, conv_u[:, j, 0:SEQ], ACT.Identity, bias=p("dw_b", m),
                               scale=p("dw_w", m * TAPS)).then_inc(c_tap, 1)

            with act.Fori(0, KT // 2) as i:
                for j in range(2):
                    conv_unit(2 * i + j, j, 2 * i + j)

            act.wait_ge(mean_mm, 1)
            act.activation(ln_mean, bank[NORM][:, :], ACT.Copy, scale=1.0 / D).then_inc(mean_sb, 1)
            for k in range(KT):
                act.wait_ge(xc_done, k + 1)
                if k >= 2:
                    act.wait_ge(var_mm, k - 1)
                act.activation(ln_sq[:, k % 2, :], conv_c[:, k, :], ACT.Square).then_inc(xc_sq, 1)
            act.wait_ge(var_mm, KT)
            act.activation(ms, bank[NORM][:, :], ACT.Sqrt, bias=eps, scale=1.0 / D).then_inc(var_ms, 1)
            for k in range(KT):
                act.wait_ge(y_n, k + 1)
                act.activation(conv_c[:, k, :], conv_c[:, k, :], ACT.Silu, bias=p("ln_b", k),
                               scale=p("ln_g", k)).then_inc(y_s, 1)
                act.wait_ge(y_s, k + 1)
                act.activation(act_hi[:, k, :], conv_c[:, k, :], ACT.Copy).then_inc(a_hi_done, 1)

            def residual_units(first, count, stage, last=False):
                for u in range(count):
                    n = first + u
                    if n + 1 in row_gain:
                        split_gained(n + 1, range(4))
                    elif n + 1 < UNITS and n != FIRST["wo"]:
                        split_weights(n + 1, (n + 1) % RING)
                    for j in range(2):
                        if stage is not None:
                            k = 2 * u + j
                            act.wait_ge(x_new, SQ[stage] - KT + k + 1)
                            xg_tile(stage, k)

            residual_units(FIRST["pw2"], KT // 2, "ffn0")

            def ffn(layer, next_stage):
                done = 0
                for c, count in enumerate(CHUNKS):
                    n0 = FIRST["in", layer, c]
                    f0 = layer * FT + sum(CHUNKS[:c])
                    t0 = sum(CHUNKS[:c])
                    if c == 0:
                        split_weights(n0 + 1, 1)
                        mean_square(1 if layer == 0 else 3)

                    def unit(i, j, split=True):
                        n, f, t = n0 + j + 2 * i, f0 + j + 2 * i, t0 + j + 2 * i
                        if split:
                            split_weights(n + 1, 1 - j)
                        for s in range(2):
                            act.wait_ge(u_done, 2 * f + s + 1)
                            act.wait_ge(a_lo_done, KT + f + 1)
                            at = layer * 2 * FT + s * FT
                            act.activation(ffn_t[:, 2 * j + s, :], ffn_u[:, 2 * j + s, FTAPS - 1:UP], ACT.Identity,
                                           bias=p("ffn_dw_b", at + t),
                                           scale=p("ffn_dw_w", (at + t) * FTAPS + FTAPS - 1)).then_inc(tap0, 1)
                        act.wait_ge(taps_done, 2 * f + 1)
                        act.activation(ffn_t[:, 2 * j, :], ffn_t[:, 2 * j, :], ACT.Silu).then_inc(silu_done, 1)
                        act.wait_ge(prod_done, f + 1)
                        act.activation(act_hi[:, bass.ds(t - t0, 1), :], ffn_t[:, 2 * j + 1, :].rearrange("p (a b) -> p a b", a=1),
                                       ACT.Copy).then_inc(a_hi_done, 1)

                    if c == 0:
                        unit(0, 0, split=False)
                        unit(0, 1)
                        with act.Fori(1, count // 2) as i:
                            for j in range(2):
                                unit(i, j)
                    else:
                        with act.Fori(0, count // 2) as i:
                            for j in range(2):
                                unit(i, j)
                    residual_units(FIRST["out", layer, c], KT // 2, next_stage if c == 2 else None)

            ffn(0, "kqv")

            def dense(g, q):
                if g == GROUPS:
                    if q == 0:
                        split_weights(FIRST["wo"] + 1, 1)
                    return
                n = FIRST["kqv"] + 3 * g + q // 8
                if n + 1 == FIRST["wo"]:
                    if q % 8 == 0:
                        act.sem_inc(w_hi_done, 3 * GROUPS)
                        split_weights(n + 1, (n + 1) % RING)
                elif q % 8 < 4:
                    split_gained(n + 1, [q % 8])
                if q % 2 == 0:
                    return
                q //= 2
                u, part = divmod(q, 4)
                if g == 0 and q == 1:
                    act.wait_ge(norm_mm, 3)
                    act.activation(rs_t_in, bank[NORM][:, 0:TB], ACT.Sqrt, bias=eps, scale=1.0 / D).then_inc(norm_ms, 1)
                if u == 2 and part % 2 == 1:
                    act.wait_ge(tiles, TILE0 + 2 * n + part // 2 + 1)
                    for b in (part - 1, part):
                        got = act.activation(v_hi[:, g % 2, b, :], bank[2 * (n % RING) + part // 2][:, (b % 2) * 2 * P:(b % 2 + 1) * 2 * P],
                                             ACT.Copy, scale=rs_t[:, b:b + 1])
                    got.then_inc(v_hi_s, 1)

            def d_hi(h, n):
                act.wait_ge(dt_done, 3 * h + n + 1)
                for b in SETS[n]:
                    w = (b + 1) * P
                    got = act.activation(dT_hi[:, TRI[b]:TRI[b] + w], bank[6][:, COLUMN[b]:COLUMN[b] + w], ACT.Copy)
                got.then_inc(dT_h, 1)

            def exps(h, n):
                for c in range(2):
                    act.wait_ge(m_done, component(h, n, c))
                    for b in SETS[n]:
                        w = (b + 1) * P
                        act.activation(prob[:, n % 2, c, COLUMN[b]:COLUMN[b] + w], bank[4 + c][:, COLUMN[b]:COLUMN[b] + w],
                                       ACT.Exp, bias=neg_max[:, 2 * b + c:2 * b + c + 1],
                                       accum_out=prob_sum[:, 2 * b + c:2 * b + c + 1]).then_inc(e_done, 1)

            def step(h, name):
                if name == "turn K":
                    act.wait_ge(turned, 2 * h + 1)
                    act.activation(kT_hi[:, :], bank[7][:, :], ACT.Copy, scale=p("k_norm_g")).then_inc(turned_hi, 1)
                elif name == "turn Q":
                    act.wait_ge(turned, 2 * h + 2)
                    act.activation(qT_hi[:, :], bank[6][:, :], ACT.Copy, scale=gq8).then_inc(turned_hi, 1)
                elif name == "output":
                    act.wait_ge(o_done, h + 1)
                    for b in range(TB):
                        got = act.activation(o_sb[:, b, :], bank[7][:, b * VD:(b + 1) * VD], ACT.Square,
                                             accum_out=o_ms[:, b:b + 1])
                    got.then_inc(o_squared, 1)
                elif name == "turn output":
                    act.wait_ge(oT_done, h + 1)
                    act.activation(act_hi[:, h, :], bank[7][:, :], ACT.Copy, scale=gsub).then_inc(oT_h, 1)
                elif name.startswith("score"):
                    exps(h, LETTER[name[-1]])
                elif name.startswith("turn"):
                    d_hi(h, LETTER[name[-1]])

            attention_schedule(dense, step)
            residual_units(FIRST["wo"], KT // 2, "ffn1")
            ffn(1, None)

        @block.vector
        def _(dve):
            own = Own(dve, dve_own)
            sub = ALU.subtract

            def split_weights(n, j):
                dve.wait_ge(w_hi_done, n + 1)
                dve.tensor_tensor(w_lo[:, j, :], w_raw[:, j, :], w_hi[:, j, :].bitcast(F32), sub).then_inc(w_lo_done, 1)

            def split_gained(n, parts):
                j = n % RING
                for k in (2 * part + i for part in parts for i in range(2)):
                    cols = slice(k * 2 * P, (k + 1) * 2 * P)
                    dve.wait_ge(w_hi_part, 4 * (n - FIRST["kqv"]) + k // 2 + 1)
                    got = dve.scalar_tensor_tensor(out=w_lo[:, j, cols], in0=w_raw[:, j, cols], scalar=p(row_gain[n], k),
                                                   in1=w_hi[:, j, cols].bitcast(F32), op0=ALU.mult, op1=sub)
                if k == KT - 1:
                    got.then_inc(w_lo_done, 1)

            def xg_lo_tile(stage, k):
                scale = p(gains[stage][0], gains[stage][1] + k) if gains[stage] else 1.0
                dve.wait_ge(xg_hi_done, XG[stage] + k + 1)
                dve.scalar_tensor_tensor(out=xg_lo[:, k, :], in0=x[:, k, :], scalar=scale,
                                         in1=xg_hi[:, k, :].bitcast(F32), op0=ALU.mult, op1=sub).then_inc(xg_lo_done, 1)

            own.mark(dve.memset(ones[:, :], 1.0))
            own.mark(dve.memset(conv_u[:, :, 0:TAPS - 1], 0.0))
            n = own.mark(dve.memset(eps, EPS))
            own.wait(n)
            dve.sem_inc(banks_free, RING)
            dve.sem_inc(a_lo_done, 2)
            dve.sem_inc(sq_added, 2)
            dve.sem_inc(dve_const, 1)
            dve.wait_ge(par_in, 16)
            dve.wait_ge(lam_in_sem, 16)
            own.wait(own.mark(dve.tensor_tensor(lam_prod, lam_in[:, 0:2], lam_in[:, 2:4], ALU.mult)))
            dve.tensor_reduce(lam_sum, lam_prod, AX_X, ALU.add).then_inc(lam_summed, 1)
            own.mark(dve.tensor_scalar(gq8, p("q_norm_g"), HD ** -0.5, None, ALU.mult))
            own.mark(dve.tensor_scalar(gsub, p("subln_g"), 1.0 - LAM_INIT, None, ALU.mult))
            dve.wait_ge(lam_exped, 1)
            own.wait(own.mark(dve.tensor_tensor(neg_lam, lam_exp[:, 1:2], lam_exp[:, 0:1], sub)))
            own.wait(own.mark(dve.tensor_scalar(neg_lam, neg_lam, LAM_INIT, None, sub)))
            for k in range(KT):
                dve.wait_ge(x_in[k], 16)
                xg_lo_tile("conv", k)
                if k == 1:
                    split_weights(0, 0)

            def inverse_root(n):
                dve.wait_ge(norm_ms, n)
                dve.reciprocal(rs, ms).then_inc(norm_rs, 1)
                dve.wait_ge(norm_rs, n)

            inverse_root(1)
            PER = TAPS
            with own.loop(KT // 2, 2 * PER) as i:
                for j in range(2):
                    m = 2 * i + j
                    dve.wait_ge(tiles, TILE0 + 2 * m + 1)
                    a = own.mark(dve.tensor_tensor(conv_a[:, 0, :], bank[2 * j][:, :], rs, ALU.mult))
                    split_weights(m + 1, 1 - j)
                    dve.wait_ge(tiles, TILE0 + 2 * m + 2)
                    dve.tensor_tensor(conv_a[:, 1, :], bank[2 * j + 1][:, :], rs, ALU.mult).then_inc(c_g, 1)
                    own.wait(a)
                    dve.wait_ge(c_sig, m + 1)
                    dve.sem_inc(banks_free, 1)
                    dve.scalar_tensor_tensor(out=conv_u[:, j, TAPS - 1:CP], in0=conv_a[:, 0, :], scalar=p("pw1_b", m),
                                             in1=conv_a[:, 1, :], op0=ALU.add, op1=ALU.mult).then_inc(c_u, 1)
                    dve.wait_ge(c_u, m + 1)
                    last = [None, None]
                    c_tile = conv_c[:, bass.ds(m, 1), :].rearrange("p a b -> p (a b)")
                    chain = [conv_b, c_tile]
                    for t in range(1, TAPS):
                        which = t % 2
                        src = conv_u[:, j, t:t + SEQ]
                        w = p("dw_w", m * TAPS + t)
                        if t == 1:
                            last[1] = own.mark(dve.tensor_scalar(chain[1], src, w, None, ALU.mult))
                            continue
                        if t == 2:
                            dve.wait_ge(c_tap, m + 1)
                        if last[which] is not None:
                            own.wait(last[which])
                        last[which] = own.mark(dve.scalar_tensor_tensor(out=chain[which], in0=src, scalar=w,
                                                                        in1=chain[which], op0=ALU.mult, op1=ALU.add))
                    own.wait(last[0])
                    own.wait(last[1])
                    dve.tensor_tensor(c_tile, chain[1], chain[0], ALU.add).then_inc(c_done, 1)

            dve.wait_ge(mean_sb, 1)
            for k in range(KT):
                dve.tensor_tensor(conv_c[:, k, :], conv_c[:, k, :], ln_mean, sub).then_inc(xc_done, 1)
            dve.wait_ge(var_ms, 1)
            dve.reciprocal(rs, ms).then_inc(var_rs, 1)
            dve.wait_ge(var_rs, 1)
            dve.wait_ge(xc_done, KT)
            for k in range(KT + 1):
                if k < KT:
                    dve.tensor_tensor(conv_c[:, k, :], conv_c[:, k, :], rs, ALU.mult).then_inc(y_n, 1)
                if k >= 1:
                    dve.wait_ge(a_hi_done, k)
                    dve.tensor_tensor(act_lo[:, k - 1, :], conv_c[:, k - 1, :], act_hi[:, k - 1, :].bitcast(F32),
                                      sub).then_inc(a_lo_done, 1)

            def residual_units(first, stage, bias=None):
                for u in range(KT // 2):
                    n = first + u
                    for j in range(2):
                        k = 2 * u + j
                        dve.wait_ge(tiles, TILE0 + 2 * n + j + 1)
                        b = bank[2 * (n % RING) + j][:, :]
                        if bias is None:
                            new = dve.tensor_tensor(x[:, k, :], b, x[:, k, :], ALU.add)
                        else:
                            new = dve.scalar_tensor_tensor(out=x[:, k, :], in0=b, scalar=p(bias, k), in1=x[:, k, :],
                                                           op0=ALU.add, op1=ALU.add)
                        if stage is not None:
                            new.then_inc(x_new, 1)
                        else:
                            own.mark(new)
                        if j == 0 and n + 1 in row_gain:
                            split_gained(n + 1, range(4))
                        elif j == 0 and n + 1 < UNITS and n != FIRST["wo"]:
                            split_weights(n + 1, (n + 1) % RING)
                        if stage not in (None, "out"):
                            xg_lo_tile(stage, k)
                    if stage is not None:
                        dve.wait_ge(x_new, (4 * KT if stage == "out" else SQ[stage]) - KT + k + 1)
                    else:
                        own.wait(own.count)
                    dve.sem_inc(banks_free, 1)

            residual_units(FIRST["pw2"], "ffn0", "pw2_b")

            def ffn(layer, next_stage):
                own.wait(own.mark(dve.memset(ffn_u[:, :, 0:FTAPS - 1], 0.0)))
                inverse_root(2 if layer == 0 else 4)
                for c, count in enumerate(CHUNKS):
                    n0 = FIRST["in", layer, c]
                    f0 = layer * FT + sum(CHUNKS[:c])
                    t0 = sum(CHUNKS[:c])
                    with own.loop(count // 2, 4) as i:
                        for j in range(2):
                            n, f, t = n0 + j + 2 * i, f0 + j + 2 * i, t0 + j + 2 * i
                            for s in range(2):
                                dve.wait_ge(tiles, TILE0 + 2 * n + s + 1)
                                u = ffn_u[:, 2 * j + s, :]
                                v = ffn_t[:, 2 * j + s, :]
                                w = (layer * 2 * FT + s * FT + t) * FTAPS
                                dve.tensor_tensor(u[:, FTAPS - 1:UP], bank[2 * j + s][:, :], rs, ALU.mult).then_inc(u_done, 1)
                                if s == 0:
                                    split_weights(n + 1, 1 - j)
                                dve.wait_ge(u_done, 2 * f + s + 1)
                                if s == 1:
                                    dve.sem_inc(banks_free, 1)
                                dve.wait_ge(tap0, 2 * f + s + 1)
                                own.wait(own.mark(dve.scalar_tensor_tensor(
                                    out=v, in0=u[:, 1:1 + SEQ], scalar=p("ffn_dw_w", w + 1), in1=v,
                                    op0=ALU.mult, op1=ALU.add)))
                                dve.scalar_tensor_tensor(out=v, in0=u[:, 0:SEQ], scalar=p("ffn_dw_w", w), in1=v,
                                                         op0=ALU.mult, op1=ALU.add).then_inc(taps_done, 1)
                            dve.wait_ge(taps_done, 2 * f + 2)
                            dve.wait_ge(silu_done, f + 1)
                            dve.tensor_tensor(v, v, ffn_t[:, 2 * j, :], ALU.mult).then_inc(prod_done, 1)
                            dve.wait_ge(a_hi_done, KT + f + 1)
                            hi, lo = act_hi, act_lo
                            dve.tensor_tensor(lo[:, bass.ds(t - t0, 1), :], v.rearrange("p (a b) -> p a b", a=1),
                                              hi[:, bass.ds(t - t0, 1), :].bitcast(F32), sub).then_inc(a_lo_done, 1)
                    residual_units(FIRST["out", layer, c], next_stage if c == 2 else None)

            ffn(0, "kqv")
            def dense(g, q):
                if g == GROUPS:
                    if q == 3:
                        split_weights(FIRST["wo"] + 1, 1)
                    return
                n = FIRST["kqv"] + 3 * g + q // 8
                if n + 1 == FIRST["wo"]:
                    if q % 8 == 4:
                        split_weights(n + 1, (n + 1) % RING)
                elif 2 <= q % 8 < 6:
                    split_gained(n + 1, [q % 8 - 2])
                if q % 2 == 0:
                    return
                q //= 2
                u, part = divmod(q, 4)
                if part % 2 == 1:
                    if g == 0 and q == 1:
                        dve.wait_ge(norm_ms, 3)
                        dve.reciprocal(rs_t, rs_t_in).then_inc(norm_rs, 1)
                        dve.wait_ge(norm_rs, 3)
                    if u == 2:
                        dve.wait_ge(v_hi_s, 2 * g + part // 2 + 1)
                    else:
                        dve.wait_ge(tiles, TILE0 + 2 * n + part // 2 + 1)
                    for b in (part - 1, part):
                        of = bank[2 * (n % RING) + part // 2][:, (b % 2) * 2 * P:(b % 2 + 1) * 2 * P]
                        if u == 2:
                            got = dve.scalar_tensor_tensor(out=v_lo[:, g % 2, b, :], in0=of, scalar=rs_t[:, b:b + 1],
                                                           in1=v_hi[:, g % 2, b, :].bitcast(F32), op0=ALU.mult, op1=sub)
                        else:
                            got = dve.tensor_scalar((k_sb, q_sb)[u][:, g % 2, b, :], of, rs_t[:, b:b + 1], None, ALU.mult)
                    got.then_inc(kqv_half, 1)
                    if part == 3:
                        dve.wait_ge(kqv_half, 6 * g + 2 * u + 2)
                        dve.sem_inc(banks_free, 1)
                if q in (5, 9):
                    u = q // 8
                    dve.wait_ge(kq_squared, 4 * g + 2 * u + 2)
                    if (g, u) > (0, 0):
                        dve.wait_ge(kq_normed, 2 * g + u)
                    dve.tensor_reduce(stat, kq_sq[:, :, :].rearrange("p b (c d) -> p (b c) d", c=4), AX_X,
                                      ALU.add).then_inc(kq_summed, 1)

            def d_lo(h, n):
                dve.wait_ge(dT_h, 3 * h + n + 1)
                for b in SETS[n]:
                    w = (b + 1) * P
                    got = dve.tensor_tensor(dT_lo[:, TRI[b]:TRI[b] + w], bank[6][:, COLUMN[b]:COLUMN[b] + w],
                                            dT_hi[:, TRI[b]:TRI[b] + w].bitcast(F32), sub)
                got.then_inc(dT_l, 1)

            def maxima(h, n):
                for c in range(2):
                    dve.wait_ge(s_done, component(h, n, c))
                    for b in SETS[n]:
                        dve.tensor_reduce(neg_max[:, 2 * b + c:2 * b + c + 1],
                                          bank[4 + c][:, COLUMN[b]:COLUMN[b] + (b + 1) * P],
                                          AX_X, ALU.max, negate=True).then_inc(m_done, 1)

            def differ(h, n):
                dve.wait_ge(e_done, component(h, n, 1))
                for b in SETS[n]:
                    w = slice(COLUMN[b], COLUMN[b] + (b + 1) * P)
                    own.wait(own.mark(dve.reciprocal(inv[:, 2 * b:2 * b + 2], prob_sum[:, 2 * b:2 * b + 2])))
                    own.wait(own.mark(dve.tensor_scalar(prob[:, n % 2, 1, w], prob[:, n % 2, 1, w],
                                                        inv[:, 2 * b + 1:2 * b + 2], neg_lam, ALU.mult, ALU.mult)))
                    dve.scalar_tensor_tensor(out=prob[:, n % 2, 0, w], in0=prob[:, n % 2, 0, w],
                                             scalar=inv[:, 2 * b:2 * b + 1], in1=prob[:, n % 2, 1, w],
                                             op0=ALU.mult, op1=ALU.add).then_inc(d_done, 1)

            def step(h, name):
                if name == "turn K":
                    dve.wait_ge(turned_hi, 2 * h + 1)
                    dve.scalar_tensor_tensor(out=kT_lo[:, :], in0=bank[7][:, :], scalar=p("k_norm_g"),
                                             in1=kT_hi[:, :].bitcast(F32), op0=ALU.mult, op1=sub).then_inc(turned_lo, 1)
                elif name == "turn Q":
                    dve.wait_ge(turned_hi, 2 * h + 2)
                    dve.scalar_tensor_tensor(out=qT_lo[:, :], in0=bank[6][:, :], scalar=gq8,
                                             in1=qT_hi[:, :].bitcast(F32), op0=ALU.mult, op1=sub).then_inc(turned_lo, 1)
                elif name == "norm output":
                    dve.wait_ge(o_root, h + 1)
                    for b in range(TB):
                        got = dve.tensor_scalar(o_sb[:, b, :], bank[7][:, b * VD:(b + 1) * VD], o_rs[:, b:b + 1],
                                                None, ALU.mult)
                    got.then_inc(o_normed, 1)
                elif name == "turn output":
                    dve.wait_ge(oT_h, h + 1)
                    dve.scalar_tensor_tensor(out=act_lo[:, h, :], in0=bank[7][:, :], scalar=gsub,
                                             in1=act_hi[:, h, :].bitcast(F32), op0=ALU.mult, op1=sub).then_inc(oT_l, 1)
                elif name == "score A":
                    maxima(h, 0)
                elif name == "score B":
                    differ(h, 0)
                    maxima(h, 1)
                elif name == "turn A":
                    d_lo(h, 0)
                elif name == "score C":
                    differ(h, 1)
                    maxima(h, 2)
                elif name == "turn B":
                    d_lo(h, 1)
                    differ(h, 2)
                elif name == "turn C":
                    d_lo(h, 2)

            attention_schedule(dense, step)
            residual_units(FIRST["wo"], "ffn1")
            ffn(1, "out")

        @block.tensor
        def _(pe):
            def weights(w, j, tiles_k, k, m):
                return w[:, j, (k * 2 + m) * P:(k * 2 + m + 1) * P]

            def passes(out, j, m, k, hi, lo, count):
                for s, (w, v) in enumerate(((w_hi, hi), (w_hi, lo), (w_lo, hi))):
                    got = pe.matmul(out, weights(w, j, count, k, m), v[:, k, :], start=(k == 0 and s == 0),
                                    stop=(k == count - 1 and s == 2), skip_group_check=True)
                return got

            def begin(n):
                pe.wait_ge(w_lo_done, n + 1)
                pe.wait_ge(banks_free, n + 1)

            def unit(n, j, hi, lo, count, late=0, ready=None, middle=None):
                begin(n)
                early = count - late
                for m in range(2):
                    for k in range(early):
                        if ready and m == 0:
                            ready(k)
                        got = passes(bank[2 * j + m][:, :], j, m, k, hi, lo, count)
                    if not late:
                        got.then_inc(tiles, 1)
                for m in range(2):
                    for k in range(early, count):
                        if ready and m == 0:
                            ready(k)
                        got = passes(bank[2 * j + m][:, :], j, m, k, hi, lo, count)
                    if late:
                        got.then_inc(tiles, 1)
                    if middle and m == 0:
                        middle()

            def square_sum(stage_n):
                pe.wait_ge(sq_added, 2 + KT * (stage_n + 1))
                pe.matmul(bank[NORM][:, :], ones[:, :], sq_sum, start=True, stop=True).then_inc(norm_mm, 1)

            def xg_ready(stage):
                return lambda k: pe.wait_ge(xg_lo_done, XG[stage] + k + 1)

            pe.wait_ge(dve_const, 1)
            pe.wait_ge(const_ready, 4)
            pe.sem_inc(tiles, TILE0)
            unit(0, 0, xg_hi, xg_lo, KT, 4, xg_ready("conv"), lambda: square_sum(0))
            unit(1, 1, xg_hi, xg_lo, KT)
            with pe.Fori(1, KT // 2) as i:
                for j in range(2):
                    unit(2 * i + j, j, xg_hi, xg_lo, KT)
            pe.wait_ge(c_added, KT)
            pe.matmul(bank[NORM][:, :], ones[:, :], ln_sum, start=True, stop=True).then_inc(mean_mm, 1)
            pe.wait_ge(mean_sb, 1)
            for k in range(KT):
                pe.wait_ge(xc_sq, k + 1)
                pe.matmul(bank[NORM][:, :], ones[:, :], ln_sq[:, k % 2, :], start=k == 0, stop=k == KT - 1).then_inc(var_mm, 1)

            def residual_units(first, hi, lo, count, late, ready):
                unit(first, 0, hi, lo, count, late, ready)
                unit(first + 1, 1, hi, lo, count)
                unit(first + 2, 0, hi, lo, count)
                unit(first + 3, 1, hi, lo, count)

            residual_units(FIRST["pw2"], act_hi, act_lo, KT, 2, lambda k: pe.wait_ge(a_lo_done, 2 + k + 1))

            def ffn(layer):
                hi, lo = xg_hi, xg_lo
                for c, count in enumerate(CHUNKS):
                    n0 = FIRST["in", layer, c]
                    i0 = 0
                    if c == 0:
                        unit(n0, 0, hi, lo, KT, 2, xg_ready(f"ffn{layer}"), lambda: square_sum(1 if layer == 0 else 3))
                        unit(n0 + 1, 1, hi, lo, KT)
                        i0 = 1
                    with pe.Fori(i0, count // 2) as i:
                        for j in range(2):
                            unit(n0 + 2 * i + j, j, hi, lo, KT)
                    a0 = 2 + KT + layer * FT + sum(CHUNKS[:c])
                    residual_units(FIRST["out", layer, c], act_hi, act_lo, count, 2, lambda k: pe.wait_ge(a_lo_done, a0 + k + 1))

            ffn(0)

            def dense(g, q):
                if g == GROUPS:
                    tile, k = divmod(q, 5) if q < 20 else (q - 20, 5)
                    if q in (0, 10):
                        begin(FIRST["wo"] + tile // 2)
                    pe.wait_ge(oT_l, k + 1)
                    passes(bank[tile][:, :], tile // 2, tile % 2, k, act_hi, act_lo, KT)
                    return
                u, b = divmod(q // 2, 4)
                n = FIRST["kqv"] + 3 * g + u
                j = n % RING
                if q % 8 == 0:
                    begin(n)
                out = bank[2 * j + b // 2][:, (b % 2) * 2 * P:(b % 2 + 1) * 2 * P]
                for k in range(q % 2 * 4, q % 2 * 4 + 4):
                    if g == 0 and q < 2:
                        xg_ready("kqv")(k)
                    for s, (v, w) in enumerate(((xg_hi, w_hi), (xg_hi, w_lo), (xg_lo, w_hi))):
                        got = pe.matmul(out, v[:, k, b * P:(b + 1) * P], w[:, j, k * 2 * P:(k + 1) * 2 * P],
                                        start=(k == 0 and s == 0), stop=(k == KT - 1 and s == 2),
                                        skip_group_check=True)
                if q % 4 == 3:
                    got.then_inc(tiles, 1)
                if g == 0 and q == 1:
                    pe.wait_ge(sq_added, 2 + 3 * KT)
                    for t in range(TB):
                        last = pe.matmul(bank[NORM][:, t:t + 1], sq_sum[:, t * P:(t + 1) * P], ones[:, 0:1],
                                         start=True, stop=True, skip_group_check=True)
                    last.then_inc(norm_mm, 1)

            def turn(h, n):
                pe.wait_ge(d_done, 4 * h + PLACE[SETS[n][-1]] + 1)
                for b in SETS[n]:
                    for k in range(b + 1):
                        at = COLUMN[b] + k * P
                        got = pe.transpose(bank[6][:, at:at + P], prob[:, n % 2, 0, at:at + P], ident[:, :])
                got.then_inc(dt_done, 1)

            def scores(h, n):
                if 8 * h + 2 * PLACE[SETS[n][0]]:
                    pe.wait_ge(e_done, 8 * h + 2 * PLACE[SETS[n][0]])
                for c in range(2):
                    for b in SETS[n]:
                        out = bank[4 + c][:, COLUMN[b]:COLUMN[b] + (b + 1) * P]
                        rows = slice(c * HD, (c + 1) * HD)
                        qs = slice(b * P, (b + 1) * P)
                        for s, (q, k) in enumerate(((qT_hi, kT_hi), (qT_hi, kT_lo), (qT_lo, kT_hi))):
                            pe.matmul(out, q[rows, qs], k[rows, 0:(b + 1) * P],
                                      start=s == 0, stop=False, skip_group_check=True)
                        pe.matmul(out[:, b * P:(b + 1) * P], ident16[:, :], mask16[:, :], start=False, stop=True,
                                  skip_group_check=True).then_inc(s_done, 1)

            def step(h, name):
                g, r = divmod(h, 2)
                cols = slice(r * P, (r + 1) * P)
                if name == "turn K":
                    pe.wait_ge(kq_normed, 2 * g + 1)
                    if h >= 2:
                        pe.wait_ge(oT_l, h - 1)
                    for b in range(TB):
                        got = pe.transpose(bank[7][:, b * P:(b + 1) * P], k_sb[:, g % 2, b, cols], ident[:, :])
                    got.then_inc(turned, 1)
                elif name == "turn Q":
                    pe.wait_ge(kq_normed, 2 * g + 2)
                    if h:
                        pe.wait_ge(dT_l, 3 * h)
                    for b in range(TB):
                        got = pe.transpose(bank[6][:, b * P:(b + 1) * P], q_sb[:, g % 2, b, cols], ident[:, :])
                    got.then_inc(turned, 1)
                elif name == "output":
                    pe.wait_ge(dT_l, 3 * h + 3)
                    pe.wait_ge(turned_lo, min(2 * h + 3, 2 * HEADS))
                    for b in range(TB):
                        for k in range(b + 1):
                            at = TRI[b] + k * P
                            for n, (d, v) in enumerate(((dT_hi, v_hi), (dT_hi, v_lo), (dT_lo, v_hi))):
                                got = pe.matmul(bank[7][:, b * VD:(b + 1) * VD], d[:, at:at + P], v[:, g % 2, k, cols],
                                                start=(k == 0 and n == 0), stop=(k == b and n == 2), skip_group_check=True)
                    got.then_inc(o_done, 1)
                elif name == "turn output":
                    pe.wait_ge(o_normed, h + 1)
                    for b in range(TB):
                        got = pe.transpose(bank[7][:, b * P:(b + 1) * P], o_sb[:, b, :], ident[:, :])
                    got.then_inc(oT_done, 1)
                elif name == "score A":
                    pe.wait_ge(turned_lo, 2 * h + 2)
                    scores(h, 0)
                elif name.startswith("score"):
                    scores(h, LETTER[name[-1]])
                elif name == "turn A":
                    turn(h, 0)
                elif name == "turn B":
                    pe.wait_ge(dT_l, 3 * h + 1)
                    turn(h, 1)
                elif name == "turn C":
                    pe.wait_ge(dT_l, 3 * h + 2)
                    turn(h, 2)

            attention_schedule(dense, step)
            for tile in range(4):
                for k in (KT - 2, KT - 1):
                    pe.wait_ge(oT_l, k + 1)
                    got = passes(bank[tile][:, :], tile // 2, tile % 2, k, act_hi, act_lo, KT)
                got.then_inc(tiles, 1)
            unit(FIRST["wo"] + 2, 0, act_hi, act_lo, KT)
            unit(FIRST["wo"] + 3, 1, act_hi, act_lo, KT)
            ffn(1)


def column_tiles(v):
    return v.reshape(-1, P).T


def unit_block(w, rows, columns):
    w = w[rows[0] * P:(rows[0] + rows[1]) * P]
    w = np.concatenate([w[:, c * P:(c + 1) * P] for c in columns], axis=1)
    return w.reshape(rows[1], P, 2 * P).transpose(1, 0, 2).reshape(P, rows[1] * 2 * P)


def stream_of(i):
    blocks = []
    pairs = [(2 * u, 2 * u + 1) for u in range(KT // 2)]

    def ffn(layer):
        done = 0
        for tiles in CHUNKS:
            blocks.extend(unit_block(i["ffn_w_in"][layer], (0, KT), (done + t, FT + done + t)) for t in range(tiles))
            blocks.extend(unit_block(i["ffn_w_out"][layer], (done, tiles), c) for c in pairs)
            done += tiles

    blocks.extend(unit_block(i["conv_pw1_w"][0], (0, KT), (t, KT + t)) for t in range(KT))
    blocks.extend(unit_block(i["conv_pw2_w"][0], (0, KT), c) for c in pairs)
    ffn(0)
    blocks.extend(unit_block(w, (0, KT), c) for c in pairs for w in (i["w_k"], i["w_q"][0], i["w_v"]))
    blocks.extend(unit_block(i["w_o"][0], (0, KT), c) for c in pairs)
    ffn(1)
    return np.ascontiguousarray(np.concatenate(blocks, axis=1))


def kernel(**inputs):
    import concourse.bacc as _bacc
    from concourse.bass_utils import run_bass_kernel_spmd as _run

    i = {name: np.asarray(v) for name, v in inputs.items()}
    twice = lambda v: np.concatenate([v, v]).reshape(P, 1)
    params = np.concatenate([
        column_tiles(i["conv_norm_g"]), column_tiles(i["conv_pw1_b"]),
        i["conv_dw_w"][0].reshape(TAPS, KT, P).transpose(2, 1, 0).reshape(P, KT * TAPS),
        column_tiles(i["conv_dw_b"]), column_tiles(i["conv_ln_g"]), column_tiles(i["conv_ln_b"]),
        column_tiles(i["conv_pw2_b"]), column_tiles(i["kv_norm_g"]), column_tiles(i["attn_norm_g"]),
        column_tiles(i["ffn_norm_g"]),
        i["ffn_dw_w"].reshape(2, FTAPS, 2 * FT, P).transpose(3, 0, 2, 1).reshape(P, 2 * 2 * FT * FTAPS),
        column_tiles(i["ffn_dw_b"]), twice(i["k_norm_g"]), twice(i["q_norm_g"][0]), i["subln_g"][0].reshape(P, 1),
    ], axis=1)
    lambdas = np.stack([i["lambda_q1"][0], i["lambda_q2"][0], i["lambda_k1"][0], i["lambda_k2"][0]])
    arrays = {
        "x_t": np.ascontiguousarray(i["x"][0].T),
        "stream": stream_of(i),
        "params": np.ascontiguousarray(params),
        "lambdas": np.ascontiguousarray(np.broadcast_to(lambdas, (P, 4, HD))),
    }
    nc = _bacc.Bacc("TRN2", target_bir_lowering=False, num_devices=1)
    args = [nc.dram_tensor(n, a.shape, F32, kind="ExternalInput").ap() for n, a in arrays.items()]
    out = nc.dram_tensor("out_t", (D, SEQ), F32, kind="ExternalOutput").ap()
    trunk(nc, *args, out)
    got = _run(nc, [arrays], core_ids=[0]).results[0]["out_t"]
    return np.ascontiguousarray(got.T).reshape(1, SEQ, D)
```

```python
import math
from contextlib import ExitStack, contextmanager

import numpy as np

import concourse.bass as bass
from concourse import mybir

F32 = mybir.dt.float32
F32R = mybir.dt.float32r
BF16 = mybir.dt.bfloat16
ALU = mybir.AluOpType
ACT = mybir.ActivationFunctionType
AX_X = mybir.AxisListType.X

P = 128
D = 1024
SEQ = 512
KT = D // P
TB = SEQ // P
TAPS = 31
D_FF = 2816
FT = D_FF // P
FTAPS = 3
HEADS = 8
HD = 64
VD = 2 * HD
EPS = 1e-6
NEG = -1e30
LAM_INIT = 0.8 - 0.6 * math.exp(-0.3)
RING = 2
SLOT = KT * 2 * P
TILE0 = 2
GROUPS = HEADS // 2
CHUNKS = [KT, KT, FT - 2 * KT]
DVE_TILES = [0, 2, 3, 7]
POOL_TILES = [1, 4]
PE_TILES = [5, 6]
DIAGS = 4
PRODS = 4
PE_TAPS = 29
TAP_TURNS = PE_TAPS // DIAGS

PARAM_WIDTHS = [
    ("conv_norm_g", KT), ("pw1_b", 2 * KT), ("dw_w", KT * TAPS), ("dw_b", KT), ("ln_g", KT), ("ln_b", KT),
    ("pw2_b", KT), ("kv_norm_g", KT), ("attn_norm_g", KT), ("ffn_norm_g", 2 * KT), ("ffn_dw_w", 2 * 2 * FT * FTAPS),
    ("ffn_dw_b", 2 * 2 * FT), ("k_norm_g", 1), ("q_norm_g", 1), ("subln_g", 1),
]
PARAM_AT = {}
N_PARAMS = 0
for _name, _width in PARAM_WIDTHS:
    PARAM_AT[_name] = N_PARAMS
    N_PARAMS += _width


def unit_plan():
    first, widths = {}, []

    def phase(name, count, width=SLOT):
        first[name] = len(widths)
        widths.extend([width] * count)

    def ffn(layer):
        for c, tiles in enumerate(CHUNKS):
            phase(("in", layer, c), tiles)
            phase(("out", layer, c), KT // 2, tiles * 2 * P)

    phase("pw1", KT)
    phase("pw2", KT // 2)
    ffn(0)
    phase("kqv", GROUPS * 3)
    phase("wo", KT // 2)
    ffn(1)
    starts = [sum(widths[:n]) for n in range(len(widths) + 1)]
    return first, widths, starts


FIRST, WIDTHS, STARTS = unit_plan()
UNITS = len(WIDTHS)


SETS = [[3], [2, 0], [1]]
ORDER = [b for blocks in SETS for b in blocks]
PLACE = {b: ORDER.index(b) for b in ORDER}
COLUMN = {3: 0, 2: 0, 0: 3 * P, 1: 0}
TRI = {b: b * (b + 1) // 2 * P for b in ORDER}


def component(h, n, c):
    return 8 * h + 2 * PLACE[SETS[n][0]] + (c + 1) * len(SETS[n])


SLOTS = [["turn K"], [], ["turn C"], ["turn Q"], ["output"], ["score A"], ["norm output"], ["score B"],
         [], ["turn A", "turn output"], ["score C"], ["turn B"]]
LATE = ("turn C", "output", "norm output", "turn output")
LEAD = 20
EARLY = [divmod(n, 5) for n in range(20)] + [(0, 5), (1, 5)]
FILL = {q: EARLY[len(EARLY) * q // LEAD:len(EARLY) * (q + 1) // LEAD] for q in range(LEAD)}
FILL.update({LEAD: [(0, 6)], LEAD + 1: [(1, 6)]})
FILLED = [piece for pieces in FILL.values() for piece in pieces]
LETTER = {"A": 0, "B": 1, "C": 2}


def attention_schedule(dense, step):
    for i in range(LEAD + 24 * GROUPS):
        dense(*(divmod(i, 24) if i < 24 * GROUPS else (GROUPS, i - 24 * GROUPS)))
        if i >= LEAD:
            h, slot = divmod(i - LEAD, 12)
            for name in SLOTS[slot]:
                if name not in LATE:
                    step(h, name)
                elif h:
                    step(h - 1, name)
    for n, name in enumerate(LATE):
        step(HEADS - 1, name)
        dense(GROUPS, LEAD + n)


class Own:

    def __init__(self, engine, semaphore):
        self.engine, self.semaphore, self.base, self.count = engine, semaphore, 0, 0

    def mark(self, instruction):
        instruction.then_inc(self.semaphore, 1)
        self.count += 1
        return self.count

    def wait(self, count):
        self.engine.wait_ge(self.semaphore, self.base + count)

    @contextmanager
    def loop(self, times, each):
        before = self.base + self.count
        with self.engine.Fori(0, times) as i:
            self.base, self.count = before + each * i, 0
            yield i
            assert self.count == each, (self.count, each)
        self.base, self.count = before + each * times, 0


def trunk(nc, x_t, stream, params, lambdas, out_t):
    with ExitStack() as ctx:
        def sb(name, shape, dtype=F32):
            return ctx.enter_context(nc.sbuf_tensor(name, shape, dtype))

        def sem(name):
            return ctx.enter_context(nc.semaphore(name))

        top = -(-nc.sbuf_base // 64) * 64

        def put(name, at, shape, dtype=F32):
            size = 2 if dtype == BF16 else 4
            end = at + -(-math.prod(shape[1:]) * size // 64) * 64
            return nc.alloc_sbuf_tensor_at(name, shape, dtype, offset=at)[(slice(None),) * len(shape)], end

        x, at = put("x", top, [P, KT, SEQ])
        xg_hi, at = put("xg_hi", at, [P, KT, SEQ], F32R)
        xg_lo, at = put("xg_lo", at, [P, KT, SEQ], F32R)
        w_raw, at = put("w_raw", at, [P, RING, SLOT])
        w_hi, at = put("w_hi", at, [P, RING, SLOT], F32R)
        w_lo, at = put("w_lo", at, [P, RING, SLOT], F32R)
        par, at = put("par", at, [P, N_PARAMS])
        ident, at = put("ident", at, [P, P])
        ones, at = put("ones", at, [P, P])
        ident16, at = put("ident16", at, [P, P], BF16)
        mask16, at = put("mask16", at, [P, P], BF16)
        small, at = put("small", at, [P, 112])
        conv_area = at
        act_hi, at = put("act_hi", at, [P, KT, SEQ], F32R)
        act_lo, area = put("act_lo", at, [P, KT, SEQ], F32R)
        eps = small[:, 0:1]
        gq8 = small[:, 1:2]
        gsub = small[:, 2:3]
        neg_lam = small[:, 3:4]
        lam_sum = small[:, 4:6]
        lam_exp = small[:, 6:8]
        rs_t = small[:, 8:12]
        rs_t_in = small[:, 12:16]
        neg_max = small[:, 16:24]
        prob_sum = small[:, 24:32]
        inv = small[:, 32:40]
        o_ms = small[:, 44:48]
        o_in = small[:, 48:52]
        o_rs = small[:, 52:56]
        half = small[:, 56:57]
        stat = small[:, 60:76]
        stat_in = small[:, 76:92]

        sq, at = put("sq", area, [P, 2, SEQ])
        sq_sum, at = put("sq_sum", at, [P, SEQ])
        rs, at = put("rs", at, [P, SEQ])
        ms, own_area = put("ms", at, [P, SEQ])
        UP = SEQ + FTAPS - 1
        ffn_u, at = put("ffn_u", own_area, [P, 4, UP])
        ffn_t, at = put("ffn_t", at, [P, 4, SEQ])
        CP = SEQ + TAPS - 1
        conv_u, at = put("conv_u", conv_area, [P, KT, CP])
        diag, at = put("diag", at, [P, DIAGS, 2, P])
        prod, at = put("prod", at, [P, PRODS, SEQ])
        assert at <= area
        conv_a, at = put("conv_a", own_area, [P, 2, SEQ])
        conv_b, at = put("conv_b", at, [P, SEQ])
        conv_c, at = put("conv_c", at, [P, KT, SEQ])
        ln_sq, at = put("ln_sq", at, [P, 2, SEQ])
        ln_sum, at = put("ln_sum", at, [P, SEQ])
        lam_in, at = put("lam_in", at, [P, 4, HD])
        lam_prod, at = put("lam_prod", at, [P, 2, HD])
        v_hi, at = put("v_hi", area, [P, 2, TB, 2 * VD], F32R)
        v_lo, at = put("v_lo", at, [P, 2, TB, 2 * VD], F32R)
        k_sb, at = put("k_sb", at, [P, 2, TB, 2 * P])
        q_sb, at = put("q_sb", at, [P, 2, TB, 2 * P])
        kq_sq, at = put("kq_sq", at, [P, TB, 2 * P])
        kT_hi, at = put("kT_hi", at, [P, SEQ], F32R)
        kT_lo, at = put("kT_lo", at, [P, SEQ], F32R)
        qT_hi, at = put("qT_hi", at, [P, SEQ], F32R)
        qT_lo, at = put("qT_lo", at, [P, SEQ], F32R)
        dT_hi, at = put("dT_hi", at, [P, 10 * P], F32R)
        dT_lo, at = put("dT_lo", at, [P, 10 * P], F32R)
        prob, at = put("prob", at, [P, 2, 2, SEQ])
        o_sb, at = put("o_sb", at, [P, TB, VD])

        bank = [ctx.enter_context(nc.psum_tensor(f"bank{n}", [P, SEQ], F32)) for n in range(8)]
        CONV = (4, 5)
        VAR = 6
        NORM = 7

        par_in = sem("par_in")
        lam_in_sem = sem("lam_in")
        x_in = [sem(f"x_in{n}") for n in range(KT)]
        w_in = [sem(f"w_in{n}") for n in range(RING)]
        w_first = sem("w_first")
        w_first_hi = sem("w_first_hi")
        w_hi_done = sem("w_hi_done")
        w_hi_part = sem("w_hi_part")
        w_lo_done = sem("w_lo_done")
        tiles = sem("tiles")
        banks_free = sem("banks_free")
        const_ready = sem("const_ready")
        lam_summed = sem("lam_summed")
        lam_exped = sem("lam_exped")
        dve_own = sem("dve_own")
        pool_own = sem("pool_own")
        dve_const = sem("dve_const")
        x_new = sem("x_new")
        xg_hi_done = sem("xg_hi_done")
        xg_lo_done = sem("xg_lo_done")
        sq_done = sem("sq_done")
        sq_added = sem("sq_added")
        norm_mm = sem("norm_mm")
        norm_ms = sem("norm_ms")
        norm_rs = sem("norm_rs")
        u_done = sem("u_done")
        tap0 = sem("tap0")
        taps_done = sem("taps_done")
        silu_done = sem("silu_done")
        prod_done = sem("prod_done")
        a_hi_done = sem("a_hi_done")
        a_lo_done = sem("a_lo_done")
        c_g = sem("c_g")
        c_sig = sem("c_sig")
        c_u = sem("c_u")
        pad_done = sem("pad_done")
        c_tap = sem("c_tap")
        c_done = sem("c_done")
        pool_tap0 = sem("pool_tap0")
        prod_tap = sem("prod_tap")
        prod_added = sem("prod_added")
        diag_done = sem("diag_done")
        diag_used = sem("diag_used")
        pe_tile = sem("pe_tile")
        c_added = sem("c_added")
        mean_mm = sem("mean_mm")
        xc_done = sem("xc_done")
        xc_sq = sem("xc_sq")
        var_mm = sem("var_mm")
        var_ms = sem("var_ms")
        var_rs = sem("var_rs")
        y_n = sem("y_n")
        y_s = sem("y_s")
        kqv_half = sem("kqv_half")
        v_hi_s = sem("v_hi_s")
        kq_squared = sem("kq_squared")
        kq_summed = sem("kq_summed")
        kq_normed = sem("kq_normed")
        turned = sem("turned")
        turned_hi = sem("turned_hi")
        turned_lo = sem("turned_lo")
        s_done = sem("s_done")
        m_done = sem("m_done")
        e_done = sem("e_done")
        d_done = sem("d_done")
        dt_done = sem("dt_done")
        dT_h = sem("dT_h")
        dT_l = sem("dT_l")
        o_done = sem("o_done")
        o_squared = sem("o_squared")
        o_root = sem("o_root")
        o_normed = sem("o_normed")
        oT_done = sem("oT_done")
        oT_h = sem("oT_h")
        oT_l = sem("oT_l")
        out_s = sem("out_s")

        def p(name, n=0, width=1):
            at = PARAM_AT[name] + n
            return par[:, bass.ds(at, width)]

        gains = {"conv": ("conv_norm_g", 0), "ffn0": ("ffn_norm_g", 0), "kqv": None, "ffn1": ("ffn_norm_g", KT)}
        row_gain = {FIRST["kqv"] + 3 * g + u: ("kv_norm_g", "attn_norm_g", "kv_norm_g")[u]
                    for g in range(GROUPS) for u in range(3)}
        XG = {"conv": 0, "ffn0": KT, "kqv": 2 * KT, "ffn1": 3 * KT}
        SQ = XG

        block = ctx.enter_context(nc.Block())

        @block.sync
        def _(sp):
            sp.dma_start(par[:, :], params).then_inc(par_in, 16)
            sp.dma_start(w_raw[:, 0, 0:SLOT // 2], stream[:, 0:SLOT // 2]).then_inc(w_first, 16)
            sp.dma_start(w_raw[:, 0, SLOT // 2:SLOT], stream[:, SLOT // 2:SLOT]).then_inc(w_in[0], 16)
            for k in range(KT):
                sp.dma_start(x[:, k, :], x_t[k * P:(k + 1) * P, :]).then_inc(x_in[k], 16)
            sp.dma_start(w_raw[:, 1, :], stream[:, STARTS[1]:STARTS[2]]).then_inc(w_in[1], 16)
            sp.dma_start(lam_in, lambdas).then_inc(lam_in_sem, 16)
            n = RING
            while n < UNITS:
                width = WIDTHS[n]
                count = 1
                while n + count < UNITS and WIDTHS[n + count] == width:
                    count += 1
                assert n % RING == 0 and count % RING == 0
                with sp.Fori(0, count // RING) as i:
                    for j in range(RING):
                        sp.wait_ge(w_lo_done, n + j - RING + 1 + RING * i)
                        sp.dma_start(w_raw[:, j, 0:width],
                                     stream[:, bass.ds(STARTS[n] + j * width + RING * width * i, width)]
                                     ).then_inc(w_in[j], 16)
                n += count
            for k in range(KT):
                sp.wait_ge(x_new, 3 * KT + k + 1)
                sp.dma_start(out_t[k * P:(k + 1) * P, :], x[:, k, :]).then_inc(out_s, 16)
            sp.wait_ge(out_s, 16 * KT)

        @block.gpsimd
        def _(pool):
            own = Own(pool, pool_own)
            own.mark(pool.memset(ident[:, :], 0.0))
            own.mark(pool.memset(ident16[:, :], 0.0))
            n = own.mark(pool.memset(mask16[:, :], 0.0))
            own.wait(n)
            pool.affine_select(out=ident[:, :], in_=ident[:, :], compare_op=ALU.not_equal, fill=1.0, base=0,
                               pattern=[[-1, P]], channel_multiplier=1).then_inc(const_ready, 1)
            pool.affine_select(out=ident16[:, :], in_=ident16[:, :], compare_op=ALU.not_equal, fill=1.0, base=0,
                               pattern=[[-1, P]], channel_multiplier=1).then_inc(const_ready, 1)
            pool.affine_select(out=mask16[:, :], in_=mask16[:, :], compare_op=ALU.is_ge, fill=NEG, base=0,
                               pattern=[[-1, P]], channel_multiplier=1).then_inc(const_ready, 1)
            pool.memset(half[:, :], -0.5).then_inc(const_ready, 1)
            pool.wait_ge(const_ready, 4)

            def sum_squares(stage):
                at = SQ[stage]
                for k in range(KT):
                    pool.wait_ge(sq_done, at + k + 1)
                    if k == 0:
                        pool.tensor_copy(sq_sum, sq[:, k % 2, :]).then_inc(sq_added, 1)
                    else:
                        pool.wait_ge(sq_added, 2 + at + k)
                        pool.tensor_tensor(sq_sum, sq_sum, sq[:, k % 2, :], ALU.add).then_inc(sq_added, 1)

            def power(out, in_, shape):
                return pool.tensor_tensor(out, in_, half.broadcast_to(shape), ALU.pow)

            sum_squares("conv")
            for n, m in enumerate(POOL_TILES):
                pool.wait_ge(pool_tap0, n + 1)
                for t in range(1, TAPS):
                    at = n * (TAPS - 1) + t
                    pool.wait_ge(prod_tap, at)
                    if at > 1:
                        pool.wait_ge(prod_added, at - 1)
                    pool.tensor_tensor(conv_c[:, m, :], conv_c[:, m, :], prod[:, at % PRODS, :],
                                       ALU.add).then_inc(prod_added, 1)
            pool.wait_ge(prod_added, 2 * (TAPS - 1))
            pool.tensor_tensor(ln_sum, conv_c[:, POOL_TILES[0], :], conv_c[:, POOL_TILES[1], :], ALU.add).then_inc(c_added, 1)
            for n, k in enumerate(DVE_TILES):
                pool.wait_ge(c_done, n + 1)
                pool.wait_ge(c_added, n + 1)
                pool.tensor_tensor(ln_sum, ln_sum, conv_c[:, k, :], ALU.add).then_inc(c_added, 1)
            sum_squares("ffn0")
            sum_squares("kqv")

            def dense(g, q):
                if g == GROUPS or q % 2 == 0:
                    return
                q //= 2
                u, part = divmod(q, 4)
                if u < 2 and part % 2 == 1:
                    kq = (k_sb, q_sb)[u][:, g % 2, part - 1:part + 1, :]
                    pool.wait_ge(kqv_half, 6 * g + 2 * u + part // 2 + 1)
                    if (g, u) > (0, 0):
                        pool.wait_ge(kq_summed, 2 * g + u)
                    pool.tensor_tensor(kq_sq[:, part - 1:part + 1, :], kq, kq, ALU.mult).then_inc(kq_squared, 1)
                if q in (6, 9):
                    u = q // 8
                    pool.wait_ge(kq_summed, 2 * g + u + 1)
                    own.wait(own.mark(pool.tensor_scalar(stat_in, stat, 1.0 / HD, EPS, ALU.mult, ALU.add)))
                    own.wait(own.mark(power(stat_in, stat_in, [P, 4 * TB])))
                    kq = (k_sb, q_sb)[u][:, g % 2, :, :].rearrange("p b (c d) -> p (b c) d", c=4)
                    pool.tensor_tensor(kq, kq, stat_in.rearrange("p (a b) -> p a b", b=1).broadcast_to([P, 4 * TB, HD]),
                                       ALU.mult).then_inc(kq_normed, 1)

            def step(h, name):
                if name == "output":
                    pool.wait_ge(o_squared, h + 1)
                    own.wait(own.mark(pool.tensor_scalar(o_in, o_ms, 1.0 / VD, EPS, ALU.mult, ALU.add)))
                    power(o_rs, o_in, [P, TB]).then_inc(o_root, 1)

            attention_schedule(dense, step)
            sum_squares("ffn1")

        @block.scalar
        def _(act):
            places = iter(range(96, 112))

            def fetch_table(function):
                at = next(places)
                act.activation(small[:, at:at + 1], eps, function)

            def split_weights(n, j):
                act.wait_ge(w_in[j], (n - j) * (16 // RING) + 16)
                act.wait_ge(tiles, TILE0 + 2 * n - 2)
                act.activation(w_hi[:, j, :], w_raw[:, j, :], ACT.Copy).then_inc(w_hi_done, 1)

            def split_gained(n, parts):
                j = n % RING
                if 0 in parts:
                    act.wait_ge(w_in[j], (n - j) * (16 // RING) + 16)
                    act.wait_ge(tiles, TILE0 + 2 * n - 2)
                for k in (2 * part + i for part in parts for i in range(2)):
                    cols = slice(k * 2 * P, (k + 1) * 2 * P)
                    got = act.activation(w_hi[:, j, cols], w_raw[:, j, cols], ACT.Copy, scale=p(row_gain[n], k))
                    if k % 2:
                        got.then_inc(w_hi_part, 1)

            def xg_tile(stage, k):
                scale = p(gains[stage][0], gains[stage][1] + k) if gains[stage] else 1.0
                act.activation(xg_hi[:, k, :], x[:, k, :], ACT.Copy, scale=scale).then_inc(xg_hi_done, 1)
                act.wait_ge(sq_added, SQ[stage] + k + 1)
                act.activation(sq[:, k % 2, :], x[:, k, :], ACT.Square).then_inc(sq_done, 1)

            def mean_square(stage_n):
                fetch_table(ACT.Sqrt)
                act.wait_ge(norm_mm, stage_n + 1)
                act.activation(ms, bank[NORM][:, :], ACT.Sqrt, bias=eps, scale=1.0 / D).then_inc(norm_ms, 1)
                fetch_table(ACT.Silu if stage_n else ACT.Sigmoid)

            act.wait_ge(dve_const, 1)
            fetch_table(ACT.Sqrt)
            act.wait_ge(w_first, 16)
            act.activation(w_hi[:, 0, 0:SLOT // 2], w_raw[:, 0, 0:SLOT // 2], ACT.Copy).then_inc(w_first_hi, 1)
            act.wait_ge(w_in[0], 16)
            act.activation(w_hi[:, 0, SLOT // 2:SLOT], w_raw[:, 0, SLOT // 2:SLOT], ACT.Copy).then_inc(w_hi_done, 1)
            act.wait_ge(par_in, 16)
            for k in range(KT):
                act.wait_ge(x_in[k], 16)
                xg_tile("conv", k)
            split_weights(1, 1)
            mean_square(0)

            def multiply(m, t, slot):
                act.activation(prod[:, slot, :], conv_u[:, m, bass.ds(t, SEQ)], ACT.Copy,
                               scale=p("dw_w", m * TAPS + t)).then_inc(prod_tap, 1)

            def some_products(which):
                for n, t in which:
                    at = n * (TAPS - 1) + t
                    if at > PRODS:
                        act.wait_ge(prod_added, at - PRODS)
                    multiply(POOL_TILES[n], t, at % PRODS)

            def diagonal(t, slot):
                for n, m in enumerate(PE_TILES):
                    act.activation(diag[:, slot, n, :], ident[:, :], ACT.Copy,
                                   scale=p("dw_w", m * TAPS + t)).then_inc(diag_done, 1)

            act.wait_ge(lam_summed, 1)
            act.activation(lam_exp, lam_sum, ACT.Exp).then_inc(lam_exped, 1)
            per = 4
            products = [(n, t) for n in range(2) for t in range(1, TAPS)][:-per * (TAP_TURNS - 1)]
            for m in range(KT):
                if m == KT - 1:
                    for t in range(DIAGS):
                        diagonal(t, t)
                if m > POOL_TILES[0]:
                    share = -(-len(products) // (KT - m))
                    some = share if m == KT - 1 else share // 2
                    early, late = products[:some], products[some:share]
                    products = products[share:]
                    some_products(early)
                act.wait_ge(c_g, m + 1)
                act.activation(conv_a[:, 1, :], conv_a[:, 1, :], ACT.Sigmoid, bias=p("pw1_b", KT + m)).then_inc(c_sig, 1)
                if m not in PE_TILES:
                    act.wait_ge(c_u, m + 1)
                    act.activation(conv_c[:, m, :], conv_u[:, m, 0:SEQ], ACT.Identity, bias=p("dw_b", m),
                                   scale=p("dw_w", m * TAPS)).then_inc(pool_tap0 if m in POOL_TILES else c_tap, 1)
                if m < KT - 1:
                    split_weights(m + 2, m % RING)
                if m > POOL_TILES[0]:
                    some_products(late)

            first = TAPS - per * (TAP_TURNS - 1)
            with act.Fori(0, TAP_TURNS - 1) as i:
                for j in range(DIAGS):
                    for n, m in enumerate(PE_TILES):
                        act.wait_ge(diag_used, 2 * DIAGS * i + 2 * j + n + 1)
                        act.activation(diag[:, j, n, :], ident[:, :], ACT.Copy,
                                       scale=p("dw_w", m * TAPS + DIAGS + j + DIAGS * i)).then_inc(diag_done, 1)
                    for e in range(per * j // DIAGS, per * (j + 1) // DIAGS):
                        t = first + e + per * i
                        act.wait_ge(prod_added, TAPS - 1 - PRODS + t)
                        multiply(POOL_TILES[1], t, (TAPS - 1 + first + e) % PRODS)
            split_weights(KT + 1, 1)
            for t in range(TAP_TURNS * DIAGS, PE_TAPS):
                act.wait_ge(diag_used, 2 * (t - DIAGS) + 2)
                diagonal(t, t % DIAGS)
            fetch_table(ACT.Sqrt)

            for k in range(KT):
                act.wait_ge(xc_done, k + 1)
                if k >= 2:
                    act.wait_ge(var_mm, k - 1)
                act.activation(ln_sq[:, k % 2, :], conv_c[:, k, :], ACT.Square).then_inc(xc_sq, 1)
            act.wait_ge(var_mm, KT)
            act.activation(ms, bank[VAR][:, :], ACT.Sqrt, bias=eps, scale=1.0 / D).then_inc(var_ms, 1)
            fetch_table(ACT.Silu)
            for k in range(KT):
                act.wait_ge(y_n, k + 1)
                act.activation(conv_c[:, k, :], conv_c[:, k, :], ACT.Silu, bias=p("ln_b", k),
                               scale=p("ln_g", k)).then_inc(y_s, 1)
                act.wait_ge(y_s, k + 1)
                act.activation(act_hi[:, k, :], conv_c[:, k, :], ACT.Copy).then_inc(a_hi_done, 1)

            def residual_units(first, count, stage, ahead=1):
                for u in range(count):
                    n = first + u
                    split = n + ahead
                    if split in row_gain:
                        pass
                    elif split < UNITS and n != FIRST["pw2"] and n != FIRST["wo"] + 1:
                        if n == FIRST["wo"]:
                            split = n + 2
                        split_weights(split, split % RING)
                    if stage is not None:
                        for k in (2 * u, 2 * u + 1):
                            act.wait_ge(x_new, SQ[stage] - KT + k + 1)
                            xg_tile(stage, k)
                    if split == FIRST["kqv"]:
                        split_gained(split, range(4))

            residual_units(FIRST["pw2"], KT // 2, "ffn0")

            def ffn(layer, next_stage):
                for c, count in enumerate(CHUNKS):
                    n0 = FIRST["in", layer, c]
                    f0 = layer * FT + sum(CHUNKS[:c])
                    t0 = sum(CHUNKS[:c])
                    if c == 0:
                        split_weights(n0 + 1, 1)
                        mean_square(1 if layer == 0 else 3)

                    def unit(i, j):
                        n, f, t = n0 + j + 2 * i, f0 + j + 2 * i, t0 + j + 2 * i
                        for s in range(2):
                            act.wait_ge(u_done, 2 * f + s + 1)
                            act.wait_ge(a_lo_done, KT + f + 1)
                            at = layer * 2 * FT + s * FT
                            act.activation(ffn_t[:, 2 * j + s, :], ffn_u[:, 2 * j + s, FTAPS - 1:UP], ACT.Identity,
                                           bias=p("ffn_dw_b", at + t),
                                           scale=p("ffn_dw_w", (at + t) * FTAPS + FTAPS - 1)).then_inc(tap0, 1)
                        act.wait_ge(taps_done, 2 * f + 1)
                        act.activation(ffn_t[:, 2 * j, :], ffn_t[:, 2 * j, :], ACT.Silu).then_inc(silu_done, 1)
                        split_weights(n + 2, j)
                        act.wait_ge(prod_done, f + 1)
                        act.activation(act_hi[:, bass.ds(t - t0, 1), :], ffn_t[:, 2 * j + 1, :].rearrange("p (a b) -> p a b", a=1),
                                       ACT.Copy).then_inc(a_hi_done, 1)

                    with act.Fori(0, count // 2) as i:
                        for j in range(2):
                            unit(i, j)
                    residual_units(FIRST["out", layer, c], KT // 2, next_stage if c == 2 else None, 2)

            ffn(0, "kqv")

            def dense(g, q):
                if g == GROUPS:
                    if q == 0:
                        split_weights(FIRST["wo"] + 1, 1)
                    return
                n = FIRST["kqv"] + 3 * g + q // 8
                if n + 1 == FIRST["wo"]:
                    if q % 8 == 0:
                        act.sem_inc(w_hi_done, 3 * GROUPS)
                        split_weights(n + 1, (n + 1) % RING)
                elif q % 8 < 4:
                    split_gained(n + 1, [q % 8])
                if q % 2 == 0:
                    return
                q //= 2
                u, part = divmod(q, 4)
                if g == 0 and q == 1:
                    act.wait_ge(norm_mm, 3)
                    act.activation(rs_t_in, bank[NORM][:, 0:TB], ACT.Sqrt, bias=eps, scale=1.0 / D).then_inc(norm_ms, 1)
                if u == 2 and part % 2 == 1:
                    act.wait_ge(tiles, TILE0 + 2 * n + part // 2 + 1)
                    for b in (part - 1, part):
                        got = act.activation(v_hi[:, g % 2, b, :], bank[2 * (n % RING) + part // 2][:, (b % 2) * 2 * P:(b % 2 + 1) * 2 * P],
                                             ACT.Copy, scale=rs_t[:, b:b + 1])
                    got.then_inc(v_hi_s, 1)

            def d_hi(h, n):
                act.wait_ge(dt_done, 3 * h + n + 1)
                for b in SETS[n]:
                    w = (b + 1) * P
                    got = act.activation(dT_hi[:, TRI[b]:TRI[b] + w], bank[6][:, COLUMN[b]:COLUMN[b] + w], ACT.Copy)
                got.then_inc(dT_h, 1)

            def exps(h, n):
                for c in range(2):
                    act.wait_ge(m_done, component(h, n, c))
                    for b in SETS[n]:
                        w = (b + 1) * P
                        act.activation(prob[:, n % 2, c, COLUMN[b]:COLUMN[b] + w], bank[4 + c][:, COLUMN[b]:COLUMN[b] + w],
                                       ACT.Exp, bias=neg_max[:, 2 * b + c:2 * b + c + 1],
                                       accum_out=prob_sum[:, 2 * b + c:2 * b + c + 1]).then_inc(e_done, 1)

            def step(h, name):
                if name == "turn K":
                    act.wait_ge(turned, 2 * h + 1)
                    act.activation(kT_hi[:, :], bank[7][:, :], ACT.Copy, scale=p("k_norm_g")).then_inc(turned_hi, 1)
                elif name == "turn Q":
                    act.wait_ge(turned, 2 * h + 2)
                    act.activation(qT_hi[:, :], bank[6][:, :], ACT.Copy, scale=gq8).then_inc(turned_hi, 1)
                elif name == "output":
                    act.wait_ge(o_done, h + 1)
                    for b in range(TB):
                        got = act.activation(o_sb[:, b, :], bank[7][:, b * VD:(b + 1) * VD], ACT.Square,
                                             accum_out=o_ms[:, b:b + 1])
                    got.then_inc(o_squared, 1)
                elif name == "turn output":
                    act.wait_ge(oT_done, h + 1)
                    act.activation(act_hi[:, h, :], bank[7][:, :], ACT.Copy, scale=gsub).then_inc(oT_h, 1)
                elif name.startswith("score"):
                    exps(h, LETTER[name[-1]])
                elif name.startswith("turn"):
                    d_hi(h, LETTER[name[-1]])

            attention_schedule(dense, step)
            residual_units(FIRST["wo"], KT // 2, "ffn1")
            ffn(1, None)

        @block.vector
        def _(dve):
            own = Own(dve, dve_own)
            sub = ALU.subtract

            def split_weights(n, j):
                dve.wait_ge(w_hi_done, n + 1)
                dve.tensor_tensor(w_lo[:, j, :], w_raw[:, j, :], w_hi[:, j, :].bitcast(F32), sub).then_inc(w_lo_done, 1)

            def split_gained(n, parts):
                j = n % RING
                for k in (2 * part + i for part in parts for i in range(2)):
                    cols = slice(k * 2 * P, (k + 1) * 2 * P)
                    dve.wait_ge(w_hi_part, 4 * (n - FIRST["kqv"]) + k // 2 + 1)
                    got = dve.scalar_tensor_tensor(out=w_lo[:, j, cols], in0=w_raw[:, j, cols], scalar=p(row_gain[n], k),
                                                   in1=w_hi[:, j, cols].bitcast(F32), op0=ALU.mult, op1=sub)
                if k == KT - 1:
                    got.then_inc(w_lo_done, 1)

            def xg_lo_tile(stage, k):
                scale = p(gains[stage][0], gains[stage][1] + k) if gains[stage] else 1.0
                dve.wait_ge(xg_hi_done, XG[stage] + k + 1)
                dve.scalar_tensor_tensor(out=xg_lo[:, k, :], in0=x[:, k, :], scalar=scale,
                                         in1=xg_hi[:, k, :].bitcast(F32), op0=ALU.mult, op1=sub).then_inc(xg_lo_done, 1)

            own.mark(dve.memset(ones[:, :], 1.0))
            dve.memset(conv_u[:, :, 0:TAPS - 1], 0.0).then_inc(pad_done, 1)
            n = own.mark(dve.memset(eps, EPS))
            own.wait(n)
            dve.sem_inc(banks_free, RING)
            dve.sem_inc(a_lo_done, 2)
            dve.sem_inc(sq_added, 2)
            dve.sem_inc(dve_const, 1)
            for signal, cols in ((w_first_hi, slice(0, SLOT // 2)), (w_hi_done, slice(SLOT // 2, SLOT))):
                dve.wait_ge(signal, 1)
                got = dve.tensor_tensor(w_lo[:, 0, cols], w_raw[:, 0, cols], w_hi[:, 0, cols].bitcast(F32), sub)
            got.then_inc(w_lo_done, 1)
            dve.wait_ge(par_in, 16)
            for k in range(KT):
                dve.wait_ge(x_in[k], 16)
                xg_lo_tile("conv", k)
            split_weights(1, 1)

            def inverse_root(n):
                dve.wait_ge(norm_ms, n)
                dve.reciprocal(rs, ms).then_inc(norm_rs, 1)
                dve.wait_ge(norm_rs, n)

            inverse_root(1)
            dve.wait_ge(lam_in_sem, 16)
            own.wait(own.mark(dve.tensor_tensor(lam_prod, lam_in[:, 0:2], lam_in[:, 2:4], ALU.mult)))
            dve.tensor_reduce(lam_sum, lam_prod, AX_X, ALU.add).then_inc(lam_summed, 1)
            own.mark(dve.tensor_scalar(gq8, p("q_norm_g"), HD ** -0.5, None, ALU.mult))
            own.mark(dve.tensor_scalar(gsub, p("subln_g"), 1.0 - LAM_INIT, None, ALU.mult))
            dve.wait_ge(lam_exped, 1)
            own.wait(own.mark(dve.tensor_tensor(neg_lam, lam_exp[:, 1:2], lam_exp[:, 0:1], sub)))
            own.wait(own.mark(dve.tensor_scalar(neg_lam, neg_lam, LAM_INIT, None, sub)))
            taps = [(n, t) for n in range(len(DVE_TILES)) for t in range(1, TAPS + 1)]
            last = [None, None]

            def convolve(count):
                for n, t in taps[:count]:
                    m = DVE_TILES[n]
                    if t == TAPS:
                        own.wait(last[0])
                        own.wait(last[1])
                        last[1] = None
                        dve.tensor_tensor(conv_c[:, m, :], conv_c[:, m, :], conv_b, ALU.add).then_inc(c_done, 1)
                        continue
                    src = conv_u[:, m, t:t + SEQ]
                    w = p("dw_w", m * TAPS + t)
                    which = t % 2
                    if t == 1:
                        dve.wait_ge(c_u, m + 1)
                        if n:
                            dve.wait_ge(c_done, n)
                        last[1] = own.mark(dve.tensor_scalar(conv_b, src, w, None, ALU.mult))
                        continue
                    if t == 2:
                        dve.wait_ge(c_tap, n + 1)
                    else:
                        own.wait(last[which])
                    chain = conv_b if which else conv_c[:, m, :]
                    last[which] = own.mark(dve.scalar_tensor_tensor(out=chain, in0=src, scalar=w, in1=chain,
                                                                    op0=ALU.mult, op1=ALU.add))
                del taps[:count]

            for m in range(KT):
                j = m % RING
                dve.wait_ge(tiles, TILE0 + 2 * m + 1)
                a = own.mark(dve.tensor_tensor(conv_a[:, 0, :], bank[2 * j][:, :], rs, ALU.mult))
                if m:
                    split_weights(m + 1, 1 - j)
                    convolve(4 if m < KT - 1 else 2)
                dve.wait_ge(tiles, TILE0 + 2 * m + 2)
                dve.tensor_tensor(conv_a[:, 1, :], bank[2 * j + 1][:, :], rs, ALU.mult).then_inc(c_g, 1)
                if m:
                    convolve(2)
                own.wait(a)
                dve.wait_ge(c_sig, m + 1)
                dve.sem_inc(banks_free, 1)
                dve.scalar_tensor_tensor(out=conv_u[:, m, TAPS - 1:CP], in0=conv_a[:, 0, :], scalar=p("pw1_b", m),
                                         in1=conv_a[:, 1, :], op0=ALU.add, op1=ALU.mult).then_inc(c_u, 1)
                convolve(4)
            convolve(len(taps))
            last = [None] * len(PE_TILES)
            for t in range(PE_TAPS, TAPS):
                for n, m in enumerate(PE_TILES):
                    src, w = conv_u[:, m, t:t + SEQ], p("dw_w", m * TAPS + t)
                    if t == PE_TAPS:
                        last[n] = own.mark(dve.tensor_scalar(conv_c[:, m, :], src, w, p("dw_b", m), ALU.mult, ALU.add))
                    else:
                        own.wait(last[n])
                        last[n] = own.mark(dve.scalar_tensor_tensor(out=conv_c[:, m, :], in0=src, scalar=w,
                                                                    in1=conv_c[:, m, :], op0=ALU.mult, op1=ALU.add))
            for n, m in enumerate(PE_TILES):
                own.wait(last[n])
                dve.wait_ge(diag_used, 2 * (PE_TAPS - 1) + n + 1)
                dve.tensor_tensor(conv_c[:, m, :], bank[CONV[n]][:, :], conv_c[:, m, :], ALU.add).then_inc(pe_tile, 1)

            dve.wait_ge(mean_mm, 1)
            dve.wait_ge(c_done, len(DVE_TILES))
            dve.wait_ge(pe_tile, len(PE_TILES))
            for k in range(KT):
                dve.scalar_tensor_tensor(out=conv_c[:, k, :], in0=bank[NORM][:, :], scalar=-1.0 / D, in1=conv_c[:, k, :],
                                         op0=ALU.mult, op1=ALU.add).then_inc(xc_done, 1)
            split_weights(KT + 1, 1)
            dve.wait_ge(var_ms, 1)
            dve.reciprocal(rs, ms).then_inc(var_rs, 1)
            dve.wait_ge(var_rs, 1)
            dve.wait_ge(xc_done, KT)
            for k in range(KT + 1):
                if k < KT:
                    dve.tensor_tensor(conv_c[:, k, :], conv_c[:, k, :], rs, ALU.mult).then_inc(y_n, 1)
                if k >= 1:
                    dve.wait_ge(a_hi_done, k)
                    dve.tensor_tensor(act_lo[:, k - 1, :], conv_c[:, k - 1, :], act_hi[:, k - 1, :].bitcast(F32),
                                      sub).then_inc(a_lo_done, 1)

            def residual_units(first, stage, bias=None):
                for u in range(KT // 2):
                    n = first + u
                    if n + 1 in row_gain:
                        split_gained(n + 1, range(4))
                    elif n + 1 < UNITS and n not in (FIRST["wo"], FIRST["wo"] + 1, FIRST["pw2"]):
                        split_weights(n + 1, (n + 1) % RING)
                    for j in range(2):
                        k = 2 * u + j
                        dve.wait_ge(tiles, TILE0 + 2 * n + j + 1)
                        b = bank[2 * (n % RING) + j][:, :]
                        if bias is None:
                            new = dve.tensor_tensor(x[:, k, :], b, x[:, k, :], ALU.add)
                        else:
                            new = dve.scalar_tensor_tensor(out=x[:, k, :], in0=b, scalar=p(bias, k), in1=x[:, k, :],
                                                           op0=ALU.add, op1=ALU.add)
                        if stage is not None:
                            new.then_inc(x_new, 1)
                        else:
                            own.mark(new)
                        if stage not in (None, "out") and n != FIRST["wo"]:
                            xg_lo_tile(stage, k)
                    if stage is not None:
                        dve.wait_ge(x_new, (4 * KT if stage == "out" else SQ[stage]) - KT + k + 1)
                    else:
                        own.wait(own.count)
                    dve.sem_inc(banks_free, 1)
                    if n == FIRST["wo"]:
                        split_weights(n + 2, (n + 2) % RING)
                        for k in range(2):
                            xg_lo_tile(stage, k)

            residual_units(FIRST["pw2"], "ffn0", "pw2_b")

            def ffn(layer, next_stage):
                own.wait(own.mark(dve.memset(ffn_u[:, :, 0:FTAPS - 1], 0.0)))
                split_weights(FIRST["in", layer, 0] + 1, 1)
                inverse_root(2 if layer == 0 else 4)
                for c, count in enumerate(CHUNKS):
                    n0 = FIRST["in", layer, c]
                    f0 = layer * FT + sum(CHUNKS[:c])
                    t0 = sum(CHUNKS[:c])
                    def unit(i, j, split=True):
                        n, f, t = n0 + j + 2 * i, f0 + j + 2 * i, t0 + j + 2 * i
                        for s in range(2):
                            dve.wait_ge(tiles, TILE0 + 2 * n + s + 1)
                            u = ffn_u[:, 2 * j + s, :]
                            v = ffn_t[:, 2 * j + s, :]
                            w = (layer * 2 * FT + s * FT + t) * FTAPS
                            dve.tensor_tensor(u[:, FTAPS - 1:UP], bank[2 * j + s][:, :], rs, ALU.mult).then_inc(u_done, 1)
                            if s == 0 and split:
                                split_weights(n + 1, 1 - j)
                            dve.wait_ge(u_done, 2 * f + s + 1)
                            if s == 1:
                                dve.sem_inc(banks_free, 1)
                            dve.wait_ge(tap0, 2 * f + s + 1)
                            own.wait(own.mark(dve.scalar_tensor_tensor(
                                out=v, in0=u[:, 1:1 + SEQ], scalar=p("ffn_dw_w", w + 1), in1=v,
                                op0=ALU.mult, op1=ALU.add)))
                            dve.scalar_tensor_tensor(out=v, in0=u[:, 0:SEQ], scalar=p("ffn_dw_w", w), in1=v,
                                                     op0=ALU.mult, op1=ALU.add).then_inc(taps_done, 1)
                        dve.wait_ge(taps_done, 2 * f + 2)
                        dve.wait_ge(silu_done, f + 1)
                        dve.tensor_tensor(v, v, ffn_t[:, 2 * j, :], ALU.mult).then_inc(prod_done, 1)
                        dve.wait_ge(a_hi_done, KT + f + 1)
                        dve.tensor_tensor(act_lo[:, bass.ds(t - t0, 1), :], v.rearrange("p (a b) -> p a b", a=1),
                                          act_hi[:, bass.ds(t - t0, 1), :].bitcast(F32), sub).then_inc(a_lo_done, 1)

                    first = 0
                    if c == 0:
                        unit(0, 0, split=False)
                        unit(0, 1)
                        first = 1
                    with own.loop(count // 2 - first, 4) as i:
                        for j in range(2):
                            unit(i + first, j)
                    residual_units(FIRST["out", layer, c], next_stage if c == 2 else None)

            ffn(0, "kqv")
            def dense(g, q):
                if g == GROUPS:
                    if q == 3:
                        split_weights(FIRST["wo"] + 1, 1)
                    return
                n = FIRST["kqv"] + 3 * g + q // 8
                if n + 1 == FIRST["wo"]:
                    if q % 8 == 4:
                        split_weights(n + 1, (n + 1) % RING)
                elif 2 <= q % 8 < 6:
                    split_gained(n + 1, [q % 8 - 2])
                if q % 2 == 0:
                    return
                q //= 2
                u, part = divmod(q, 4)
                if part % 2 == 1:
                    if g == 0 and q == 1:
                        dve.wait_ge(norm_ms, 3)
                        dve.reciprocal(rs_t, rs_t_in).then_inc(norm_rs, 1)
                        dve.wait_ge(norm_rs, 3)
                    if u == 2:
                        dve.wait_ge(v_hi_s, 2 * g + part // 2 + 1)
                    else:
                        dve.wait_ge(tiles, TILE0 + 2 * n + part // 2 + 1)
                    for b in (part - 1, part):
                        of = bank[2 * (n % RING) + part // 2][:, (b % 2) * 2 * P:(b % 2 + 1) * 2 * P]
                        if u == 2:
                            got = dve.scalar_tensor_tensor(out=v_lo[:, g % 2, b, :], in0=of, scalar=rs_t[:, b:b + 1],
                                                           in1=v_hi[:, g % 2, b, :].bitcast(F32), op0=ALU.mult, op1=sub)
                        else:
                            got = dve.tensor_scalar((k_sb, q_sb)[u][:, g % 2, b, :], of, rs_t[:, b:b + 1], None, ALU.mult)
                    got.then_inc(kqv_half, 1)
                    if part == 3:
                        dve.wait_ge(kqv_half, 6 * g + 2 * u + 2)
                        dve.sem_inc(banks_free, 1)
                if q in (5, 8):
                    u = q // 8
                    dve.wait_ge(kq_squared, 4 * g + 2 * u + 2)
                    if (g, u) > (0, 0):
                        dve.wait_ge(kq_normed, 2 * g + u)
                    dve.tensor_reduce(stat, kq_sq[:, :, :].rearrange("p b (c d) -> p (b c) d", c=4), AX_X,
                                      ALU.add).then_inc(kq_summed, 1)

            def d_lo(h, n):
                dve.wait_ge(dT_h, 3 * h + n + 1)
                for b in SETS[n]:
                    w = (b + 1) * P
                    got = dve.tensor_tensor(dT_lo[:, TRI[b]:TRI[b] + w], bank[6][:, COLUMN[b]:COLUMN[b] + w],
                                            dT_hi[:, TRI[b]:TRI[b] + w].bitcast(F32), sub)
                got.then_inc(dT_l, 1)

            def maxima(h, n):
                for c in range(2):
                    dve.wait_ge(s_done, component(h, n, c))
                    for b in SETS[n]:
                        dve.tensor_reduce(neg_max[:, 2 * b + c:2 * b + c + 1],
                                          bank[4 + c][:, COLUMN[b]:COLUMN[b] + (b + 1) * P],
                                          AX_X, ALU.max, negate=True).then_inc(m_done, 1)

            def differ(h, n):
                dve.wait_ge(e_done, component(h, n, 1))
                for b in SETS[n]:
                    w = slice(COLUMN[b], COLUMN[b] + (b + 1) * P)
                    own.wait(own.mark(dve.reciprocal(inv[:, 2 * b:2 * b + 2], prob_sum[:, 2 * b:2 * b + 2])))
                    own.wait(own.mark(dve.tensor_scalar(prob[:, n % 2, 1, w], prob[:, n % 2, 1, w],
                                                        inv[:, 2 * b + 1:2 * b + 2], neg_lam, ALU.mult, ALU.mult)))
                    dve.scalar_tensor_tensor(out=prob[:, n % 2, 0, w], in0=prob[:, n % 2, 0, w],
                                             scalar=inv[:, 2 * b:2 * b + 1], in1=prob[:, n % 2, 1, w],
                                             op0=ALU.mult, op1=ALU.add).then_inc(d_done, 1)

            def step(h, name):
                if name == "turn K":
                    dve.wait_ge(turned_hi, 2 * h + 1)
                    dve.scalar_tensor_tensor(out=kT_lo[:, :], in0=bank[7][:, :], scalar=p("k_norm_g"),
                                             in1=kT_hi[:, :].bitcast(F32), op0=ALU.mult, op1=sub).then_inc(turned_lo, 1)
                elif name == "turn Q":
                    dve.wait_ge(turned_hi, 2 * h + 2)
                    dve.scalar_tensor_tensor(out=qT_lo[:, :], in0=bank[6][:, :], scalar=gq8,
                                             in1=qT_hi[:, :].bitcast(F32), op0=ALU.mult, op1=sub).then_inc(turned_lo, 1)
                elif name == "norm output":
                    dve.wait_ge(o_root, h + 1)
                    for b in range(TB):
                        got = dve.tensor_scalar(o_sb[:, b, :], bank[7][:, b * VD:(b + 1) * VD], o_rs[:, b:b + 1],
                                                None, ALU.mult)
                    got.then_inc(o_normed, 1)
                elif name == "turn output":
                    dve.wait_ge(oT_h, h + 1)
                    dve.scalar_tensor_tensor(out=act_lo[:, h, :], in0=bank[7][:, :], scalar=gsub,
                                             in1=act_hi[:, h, :].bitcast(F32), op0=ALU.mult, op1=sub).then_inc(oT_l, 1)
                elif name == "score A":
                    maxima(h, 0)
                elif name == "score B":
                    differ(h, 0)
                    maxima(h, 1)
                elif name == "turn A":
                    differ(h, 1)
                    d_lo(h, 0)
                elif name == "score C":
                    maxima(h, 2)
                elif name == "turn B":
                    differ(h, 2)
                    d_lo(h, 1)
                elif name == "turn C":
                    d_lo(h, 2)

            attention_schedule(dense, step)
            residual_units(FIRST["wo"], "ffn1")
            ffn(1, "out")

        @block.tensor
        def _(pe):
            def weights(w, j, k, m):
                return w[:, j, (k * 2 + m) * P:(k * 2 + m + 1) * P]

            def passes(out, j, m, k, hi, lo, count):
                for s, (w, v) in enumerate(((w_hi, hi), (w_hi, lo), (w_lo, hi))):
                    got = pe.matmul(out, weights(w, j, k, m), v[:, k, :], start=(k == 0 and s == 0),
                                    stop=(k == count - 1 and s == 2), skip_group_check=True)
                return got

            def begin(n):
                pe.wait_ge(w_lo_done, n + 1)
                pe.wait_ge(banks_free, n + 1)

            def unit(n, j, hi, lo, count, late=0, ready=None, between=None, at=None):
                begin(n)
                early = count - late
                order = [(m, k) for m in range(2) for k in range(early)]
                if late <= 2:
                    order += [(m, k) for m in range(2) for k in range(early, count)]
                else:
                    order += [(m, k) for k in range(early, count) for m in range(2)]
                for m, k in order:
                    if ready and m == 0:
                        ready(k)
                    got = passes(bank[2 * j + m][:, :], j, m, k, hi, lo, count)
                    if k == count - 1:
                        got.then_inc(tiles, 1)
                    if between and (m, k) == (0, at):
                        between()

            def square_sum(stage_n):
                pe.wait_ge(sq_added, 2 + KT * (stage_n + 1))
                pe.matmul(bank[NORM][:, :], ones[:, :], sq_sum, start=True, stop=True).then_inc(norm_mm, 1)

            def xg_ready(stage):
                return lambda k: pe.wait_ge(xg_lo_done, XG[stage] + k + 1)

            pe.wait_ge(dve_const, 1)
            pe.wait_ge(const_ready, 4)
            pe.sem_inc(tiles, TILE0)
            unit(0, 0, xg_hi, xg_lo, KT, 4, xg_ready("conv"), lambda: square_sum(0), KT - 2)
            unit(1, 1, xg_hi, xg_lo, KT)
            with pe.Fori(1, KT // 2) as i:
                for j in range(2):
                    unit(2 * i + j, j, xg_hi, xg_lo, KT)

            def tap(t, j, start=False, stop=False):
                for n, m in enumerate(PE_TILES):
                    pe.wait_ge(diag_done, 2 * t + n + 1)
                    pe.matmul(bank[CONV[n]][:, :], diag[:, j, n, :], conv_u[:, m, bass.ds(t, SEQ)], start=start,
                              stop=stop, skip_group_check=True).then_inc(diag_used, 1)

            pe.wait_ge(pad_done, 1)
            pe.wait_ge(c_u, PE_TILES[-1] + 1)
            for t in range(DIAGS):
                tap(t, t, start=t == 0)
            with pe.Fori(1, TAP_TURNS) as i:
                for j in range(DIAGS):
                    tap(j + DIAGS * i, j)
            for t in range(TAP_TURNS * DIAGS, PE_TAPS):
                tap(t, t % DIAGS, stop=t == PE_TAPS - 1)

            pe.wait_ge(pe_tile, len(PE_TILES))
            for n, m in enumerate(PE_TILES):
                pe.matmul(bank[NORM][:, :], ones[:, :], conv_c[:, m, :], start=n == 0, stop=False, skip_group_check=True)
            pe.wait_ge(c_added, 1 + len(DVE_TILES))
            pe.matmul(bank[NORM][:, :], ones[:, :], ln_sum, start=False, stop=True, skip_group_check=True).then_inc(mean_mm, 1)
            for k in range(KT):
                pe.wait_ge(xc_sq, k + 1)
                pe.matmul(bank[VAR][:, :], ones[:, :], ln_sq[:, k % 2, :], start=k == 0, stop=k == KT - 1).then_inc(var_mm, 1)

            def residual_units(first, hi, lo, count, late, ready):
                unit(first, 0, hi, lo, count, late, ready)
                unit(first + 1, 1, hi, lo, count)
                unit(first + 2, 0, hi, lo, count)
                unit(first + 3, 1, hi, lo, count)

            residual_units(FIRST["pw2"], act_hi, act_lo, KT, KT, lambda k: pe.wait_ge(a_lo_done, 2 + k + 1))

            def ffn(layer):
                hi, lo = xg_hi, xg_lo
                for c, count in enumerate(CHUNKS):
                    n0 = FIRST["in", layer, c]
                    i0 = 0
                    if c == 0:
                        unit(n0, 0, hi, lo, KT, 2, xg_ready(f"ffn{layer}"), lambda: square_sum(1 if layer == 0 else 3), KT - 3)
                        unit(n0 + 1, 1, hi, lo, KT)
                        i0 = 1
                    with pe.Fori(i0, count // 2) as i:
                        for j in range(2):
                            unit(n0 + 2 * i + j, j, hi, lo, KT)
                    a0 = 2 + KT + layer * FT + sum(CHUNKS[:c])
                    residual_units(FIRST["out", layer, c], act_hi, act_lo, count, 2, lambda k: pe.wait_ge(a_lo_done, a0 + k + 1))

            ffn(0)

            def dense(g, q):
                if g == GROUPS:
                    for tile, k in FILL.get(q, []):
                        if k == 0 and tile % 2 == 0:
                            begin(FIRST["wo"] + tile // 2)
                        pe.wait_ge(oT_l, k + 1)
                        passes(bank[tile][:, :], tile // 2, tile % 2, k, act_hi, act_lo, KT)
                    return
                u, b = divmod(q // 2, 4)
                n = FIRST["kqv"] + 3 * g + u
                j = n % RING
                if q % 8 == 0:
                    begin(n)
                out = bank[2 * j + b // 2][:, (b % 2) * 2 * P:(b % 2 + 1) * 2 * P]
                for k in range(q % 2 * 4, q % 2 * 4 + 4):
                    if g == 0 and q < 2:
                        xg_ready("kqv")(k)
                    for s, (v, w) in enumerate(((xg_hi, w_hi), (xg_hi, w_lo), (xg_lo, w_hi))):
                        got = pe.matmul(out, v[:, k, b * P:(b + 1) * P], w[:, j, k * 2 * P:(k + 1) * 2 * P],
                                        start=(k == 0 and s == 0), stop=(k == KT - 1 and s == 2),
                                        skip_group_check=True)
                if q % 4 == 3:
                    got.then_inc(tiles, 1)
                if g == 0 and q == 1:
                    pe.wait_ge(sq_added, 2 + 3 * KT)
                    for t in range(TB):
                        last = pe.matmul(bank[NORM][:, t:t + 1], sq_sum[:, t * P:(t + 1) * P], ones[:, 0:1],
                                         start=True, stop=True, skip_group_check=True)
                    last.then_inc(norm_mm, 1)

            def turn(h, n):
                pe.wait_ge(d_done, 4 * h + PLACE[SETS[n][-1]] + 1)
                for b in SETS[n]:
                    for k in range(b + 1):
                        at = COLUMN[b] + k * P
                        got = pe.transpose(bank[6][:, at:at + P], prob[:, n % 2, 0, at:at + P], ident[:, :])
                got.then_inc(dt_done, 1)

            def scores(h, n):
                if 8 * h + 2 * PLACE[SETS[n][0]]:
                    pe.wait_ge(e_done, 8 * h + 2 * PLACE[SETS[n][0]])
                for c in range(2):
                    for b in SETS[n]:
                        out = bank[4 + c][:, COLUMN[b]:COLUMN[b] + (b + 1) * P]
                        rows = slice(c * HD, (c + 1) * HD)
                        qs = slice(b * P, (b + 1) * P)
                        for s, (q, k) in enumerate(((qT_hi, kT_hi), (qT_hi, kT_lo), (qT_lo, kT_hi))):
                            pe.matmul(out, q[rows, qs], k[rows, 0:(b + 1) * P],
                                      start=s == 0, stop=False, skip_group_check=True)
                        pe.matmul(out[:, b * P:(b + 1) * P], ident16[:, :], mask16[:, :], start=False, stop=True,
                                  skip_group_check=True).then_inc(s_done, 1)

            def step(h, name):
                g, r = divmod(h, 2)
                cols = slice(r * P, (r + 1) * P)
                if name == "turn K":
                    pe.wait_ge(kq_normed, 2 * g + 1)
                    if h >= 2:
                        pe.wait_ge(oT_l, h - 1)
                    for b in range(TB):
                        got = pe.transpose(bank[7][:, b * P:(b + 1) * P], k_sb[:, g % 2, b, cols], ident[:, :])
                    got.then_inc(turned, 1)
                elif name == "turn Q":
                    pe.wait_ge(kq_normed, 2 * g + 2)
                    if h:
                        pe.wait_ge(dT_l, 3 * h)
                    for b in range(TB):
                        got = pe.transpose(bank[6][:, b * P:(b + 1) * P], q_sb[:, g % 2, b, cols], ident[:, :])
                    got.then_inc(turned, 1)
                elif name == "output":
                    pe.wait_ge(dT_l, 3 * h + 3)
                    pe.wait_ge(turned_lo, min(2 * h + 3, 2 * HEADS))
                    for b in range(TB):
                        for k in range(b + 1):
                            at = TRI[b] + k * P
                            for n, (d, v) in enumerate(((dT_hi, v_hi), (dT_hi, v_lo), (dT_lo, v_hi))):
                                got = pe.matmul(bank[7][:, b * VD:(b + 1) * VD], d[:, at:at + P], v[:, g % 2, k, cols],
                                                start=(k == 0 and n == 0), stop=(k == b and n == 2), skip_group_check=True)
                    got.then_inc(o_done, 1)
                elif name == "turn output":
                    pe.wait_ge(o_normed, h + 1)
                    for b in range(TB):
                        got = pe.transpose(bank[7][:, b * P:(b + 1) * P], o_sb[:, b, :], ident[:, :])
                    got.then_inc(oT_done, 1)
                elif name == "score A":
                    pe.wait_ge(turned_lo, 2 * h + 2)
                    scores(h, 0)
                elif name.startswith("score"):
                    scores(h, LETTER[name[-1]])
                elif name == "turn A":
                    turn(h, 0)
                elif name == "turn B":
                    pe.wait_ge(dT_l, 3 * h + 1)
                    turn(h, 1)
                elif name == "turn C":
                    pe.wait_ge(dT_l, 3 * h + 2)
                    turn(h, 2)

            attention_schedule(dense, step)
            pe.wait_ge(oT_l, HEADS)
            for tile in range(4):
                for k in range(KT):
                    if (tile, k) not in FILLED:
                        got = passes(bank[tile][:, :], tile // 2, tile % 2, k, act_hi, act_lo, KT)
                got.then_inc(tiles, 1)
            unit(FIRST["wo"] + 2, 0, act_hi, act_lo, KT)
            unit(FIRST["wo"] + 3, 1, act_hi, act_lo, KT)
            ffn(1)


def column_tiles(v):
    return v.reshape(-1, P).T


def unit_block(w, rows, columns):
    w = w[rows[0] * P:(rows[0] + rows[1]) * P]
    w = np.concatenate([w[:, c * P:(c + 1) * P] for c in columns], axis=1)
    return w.reshape(rows[1], P, 2 * P).transpose(1, 0, 2).reshape(P, rows[1] * 2 * P)


def stream_of(i):
    blocks = []
    pairs = [(2 * u, 2 * u + 1) for u in range(KT // 2)]

    def ffn(layer):
        done = 0
        for tiles in CHUNKS:
            blocks.extend(unit_block(i["ffn_w_in"][layer], (0, KT), (done + t, FT + done + t)) for t in range(tiles))
            blocks.extend(unit_block(i["ffn_w_out"][layer], (done, tiles), c) for c in pairs)
            done += tiles

    blocks.extend(unit_block(i["conv_pw1_w"][0], (0, KT), (t, KT + t)) for t in range(KT))
    blocks.extend(unit_block(i["conv_pw2_w"][0], (0, KT), c) for c in pairs)
    ffn(0)
    blocks.extend(unit_block(w, (0, KT), c) for c in pairs for w in (i["w_k"], i["w_q"][0], i["w_v"]))
    blocks.extend(unit_block(i["w_o"][0], (0, KT), c) for c in pairs)
    ffn(1)
    return np.ascontiguousarray(np.concatenate(blocks, axis=1))


def kernel(**inputs):
    import concourse.bacc as _bacc
    from concourse.bass_utils import run_bass_kernel_spmd as _run

    i = {name: np.asarray(v) for name, v in inputs.items()}
    twice = lambda v: np.concatenate([v, v]).reshape(P, 1)
    params = np.concatenate([
        column_tiles(i["conv_norm_g"]), column_tiles(i["conv_pw1_b"]),
        i["conv_dw_w"][0].reshape(TAPS, KT, P).transpose(2, 1, 0).reshape(P, KT * TAPS),
        column_tiles(i["conv_dw_b"]), column_tiles(i["conv_ln_g"]), column_tiles(i["conv_ln_b"]),
        column_tiles(i["conv_pw2_b"]), column_tiles(i["kv_norm_g"]), column_tiles(i["attn_norm_g"]),
        column_tiles(i["ffn_norm_g"]),
        i["ffn_dw_w"].reshape(2, FTAPS, 2 * FT, P).transpose(3, 0, 2, 1).reshape(P, 2 * 2 * FT * FTAPS),
        column_tiles(i["ffn_dw_b"]), twice(i["k_norm_g"]), twice(i["q_norm_g"][0]), i["subln_g"][0].reshape(P, 1),
    ], axis=1)
    lambdas = np.stack([i["lambda_q1"][0], i["lambda_q2"][0], i["lambda_k1"][0], i["lambda_k2"][0]])
    arrays = {
        "x_t": np.ascontiguousarray(i["x"][0].T),
        "stream": stream_of(i),
        "params": np.ascontiguousarray(params),
        "lambdas": np.ascontiguousarray(np.broadcast_to(lambdas, (P, 4, HD))),
    }
    nc = _bacc.Bacc("TRN2", target_bir_lowering=False, num_devices=1)
    args = [nc.dram_tensor(n, a.shape, F32, kind="ExternalInput").ap() for n, a in arrays.items()]
    out = nc.dram_tensor("out_t", (D, SEQ), F32, kind="ExternalOutput").ap()
    trunk(nc, *args, out)
    got = _run(nc, [arrays], core_ids=[0]).results[0]["out_t"]
    return np.ascontiguousarray(got.T).reshape(1, SEQ, D)
```
